# Optimizing a Trainium2 kernel written in Bass

```python
import math
import jax, jax.numpy as jnp
from jax import lax
import numpy as np

D_MODEL = 1024
BATCH = 1
SEQ = 512
DEPTH = 2

D_FF = 2816
HALF_STEP = 0.5
N_MOD = 9
EPS = 1e-6

SB_HEADS = 4
SB_DIM = 64
SB_BLOCK = 128
SB_W = SB_HEADS * SB_DIM

GDN_HEADS = 4
GDN_DK = 128
GDN_DV = 128
GDN_CONV = 4
GDN_CHUNK = 64
GDN_WK = GDN_HEADS * GDN_DK
GDN_WV = GDN_HEADS * GDN_DV

HG_HEADS = 4
HG_DK = 64
HG_DV = 64
HG_CHUNK = 64
HG_WK = HG_HEADS * HG_DK
HG_WV = HG_HEADS * HG_DV

D_MIX = SB_W + GDN_WV + HG_WV
IN_SIZES = (SB_W, SB_W, SB_W, GDN_WK, GDN_WK, GDN_WV, GDN_WV, GDN_HEADS, GDN_HEADS,
            HG_WK, HG_WK, HG_WV, HG_WV)
D_IN = sum(IN_SIZES)
SPLITS = tuple(int(s) for s in np.cumsum(IN_SIZES)[:-1])

kernel_name = 'hybrid_sb_gdn_hgrn2_macaron_adaln'

def _rms_norm(x, gain):
    x32 = x.astype(jnp.float32)
    y = x32 * lax.rsqrt(jnp.mean(x32 * x32, axis=-1, keepdims=True) + EPS)
    return (y * gain.astype(jnp.float32)).astype(x.dtype)

def _l2_normalize(x):
    x32 = x.astype(jnp.float32)
    return x32 * lax.rsqrt(jnp.sum(x32 * x32, axis=-1, keepdims=True) + EPS)

def _modulate(h, shift, scale):
    return h * (1.0 + scale[:, None, :]) + shift[:, None, :]

def _swiglu(h, w_in, w_out):
    gate, up = jnp.split(h @ w_in, 2, axis=-1)
    return (jax.nn.silu(gate) * up) @ w_out

def _causal_depthwise_conv(x, w):
    return lax.conv_general_dilated(
        x, w[:, None, :].astype(x.dtype), window_strides=(1,),
        padding=((GDN_CONV - 1, 0),), dimension_numbers=('NWC', 'WIO', 'NWC'),
        feature_group_count=x.shape[-1])

def _to_chunks(x, chunk):
    b, t, h = x.shape[:3]
    x = x.reshape((b, t // chunk, chunk, h) + x.shape[3:])
    x = jnp.moveaxis(x, 3, 2)
    return jnp.moveaxis(x, 1, 0)

def _from_chunks(o):
    n, b, h, c, e = o.shape
    return o.transpose(1, 0, 3, 2, 4).reshape(b, n * c, h, e)

def _stick_breaking_attention(q, k, v):
    seq, d = q.shape[1], q.shape[3]
    q = q.transpose(0, 2, 1, 3).astype(jnp.float32)
    k = k.transpose(0, 2, 1, 3).astype(jnp.float32)
    v = v.transpose(0, 2, 1, 3).astype(jnp.float32)
    scale = d ** -0.5
    outs = []
    for blk in range(seq // SB_BLOCK):
        start = blk * SB_BLOCK
        end = start + SB_BLOCK
        qb = q[:, :, start:end]
        kb = k[:, :, :end]
        vb = v[:, :, :end]
        z = jnp.einsum('bhtd,bhsd->bhts', qb, kb) * scale
        t_idx = start + jnp.arange(SB_BLOCK)[:, None]
        s_idx = jnp.arange(end)[None, :]
        causal = s_idx < t_idx
        log_keep = jnp.where(causal, -jax.nn.softplus(z), 0.0)
        between = lax.cumsum(log_keep, axis=3, reverse=True) - log_keep
        log_w = jnp.where(causal, jax.nn.log_sigmoid(z) + between, -jnp.inf)
        outs.append(jnp.einsum('bhts,bhsd->bhtd', jnp.exp(log_w), vb))
    o = jnp.concatenate(outs, axis=2)
    return o.transpose(0, 2, 1, 3)

def _gated_delta_rule(q, k, v, log_a, beta):
    c = GDN_CHUNK
    dk, dv = q.shape[-1], v.shape[-1]
    q, k, v = (_to_chunks(t, c) for t in (q, k, v))
    log_a = _to_chunks(log_a, c)
    beta = _to_chunks(beta, c)
    g = jnp.cumsum(log_a, axis=-1)
    incl = jnp.tril(jnp.ones((c, c), dtype=bool))
    strict = jnp.tril(jnp.ones((c, c), dtype=bool), k=-1)
    decay = jnp.exp(jnp.where(incl, g[..., :, None] - g[..., None, :], -jnp.inf))
    k_beta = k * beta[..., None]
    a_kk = jnp.where(strict, jnp.einsum('nbhcd,nbhsd->nbhcs', k_beta, k) * decay, 0.0)
    eye = jnp.eye(c, dtype=jnp.float32)
    rhs = jnp.concatenate([v * beta[..., None], k_beta * jnp.exp(g)[..., None]], axis=-1)
    sol = lax.linalg.triangular_solve(eye + a_kk, rhs, left_side=True, lower=True,
                                      unit_diagonal=True)
    u, w = sol[..., :dv], sol[..., dv:]
    a_qk = jnp.einsum('nbhcd,nbhsd->nbhcs', q, k) * decay
    q_dec = q * jnp.exp(g)[..., None]
    k_dec = k * jnp.exp(g[..., -1:] - g)[..., None]
    chunk_decay = jnp.exp(g[..., -1])

    def step(state, xs):
        u_c, w_c, a_c, qd_c, kd_c, cd_c = xs
        v_new = u_c - jnp.einsum('bhcd,bhde->bhce', w_c, state)
        o = jnp.einsum('bhcd,bhde->bhce', qd_c, state) + jnp.einsum('bhcs,bhse->bhce', a_c, v_new)
        state = state * cd_c[..., None, None] + jnp.einsum('bhcd,bhce->bhde', kd_c, v_new)
        return state, o

    state0 = jnp.zeros(q.shape[1:3] + (dk, dv), jnp.float32)
    _, o = lax.scan(step, state0, (u, w, a_qk, q_dec, k_dec, chunk_decay))
    return _from_chunks(o)

def _hgrn2_recurrence(q, k, v, log_f):
    c = HG_CHUNK
    dk, dv = q.shape[-1], v.shape[-1]
    q, k, v, log_f = (_to_chunks(t, c) for t in (q, k, v, log_f))
    b = jnp.cumsum(log_f, axis=-2)
    incl = jnp.tril(jnp.ones((c, c), dtype=bool))[:, :, None]

    def step(state, xs):
        q_c, k_c, v_c, b_c = xs
        pair = jnp.exp(jnp.where(incl, b_c[..., :, None, :] - b_c[..., None, :, :], -jnp.inf))
        attn = jnp.einsum('bhtd,bhtsd,bhsd->bhts', q_c, pair, k_c)
        b_last = b_c[..., -1:, :]
        o = (jnp.einsum('bhtd,bhde->bhte', q_c * jnp.exp(b_c), state)
             + jnp.einsum('bhts,bhse->bhte', attn, v_c))
        state = (jnp.exp(b_last[..., 0, :])[..., None] * state
                 + jnp.einsum('bhsd,bhse->bhde', k_c * jnp.exp(b_last - b_c), v_c))
        return state, o

    state0 = jnp.zeros(q.shape[1:3] + (dk, dv), jnp.float32)
    _, o = lax.scan(step, state0, (q, k, v, b))
    return _from_chunks(o)

def _hybrid_mixer(h, w_in, conv_w, A_log, dt_bias, sb_gain, gdn_gain, hg_gain, lower_bound, w_out):
    bsz, seq, _ = h.shape
    f32 = jnp.float32
    proj = h @ w_in
    (sb_q, sb_k, sb_v, gd_q, gd_k, gd_v, gd_z, gd_b, gd_a,
     hg_q, hg_f, hg_i, hg_g) = jnp.split(proj, SPLITS, axis=-1)

    def heads(t, n):
        return t.reshape(bsz, seq, n, -1)

    o_sb = _stick_breaking_attention(heads(sb_q, SB_HEADS), heads(sb_k, SB_HEADS),
                                     heads(sb_v, SB_HEADS))
    o_sb = _rms_norm(o_sb, sb_gain).reshape(bsz, seq, SB_W)

    qkv = jax.nn.silu(_causal_depthwise_conv(jnp.concatenate([gd_q, gd_k, gd_v], axis=-1), conv_w))
    gq, gk, gv = jnp.split(qkv, [GDN_WK, 2 * GDN_WK], axis=-1)
    gq = _l2_normalize(heads(gq, GDN_HEADS)) * (GDN_DK ** -0.5)
    gk = _l2_normalize(heads(gk, GDN_HEADS))
    gv = heads(gv, GDN_HEADS).astype(f32)
    beta = jax.nn.sigmoid(gd_b.astype(f32))
    log_a = -jnp.exp(A_log.astype(f32)) * jax.nn.softplus(gd_a.astype(f32) + dt_bias.astype(f32))
    o_gd = _gated_delta_rule(gq, gk, gv, log_a, beta)
    o_gd = (_rms_norm(o_gd, gdn_gain) * jax.nn.silu(heads(gd_z, GDN_HEADS).astype(f32)))
    o_gd = o_gd.reshape(bsz, seq, GDN_WV)

    lb = lower_bound.astype(f32)
    f_pre = hg_f.astype(f32)
    log_f = jnp.logaddexp(jnp.log(lb), jnp.log1p(-lb) + jax.nn.log_sigmoid(f_pre))
    k_in = (1.0 - lb) * jax.nn.sigmoid(-f_pre)
    q_c = jax.nn.silu(hg_q.astype(f32))
    o_hg = _hgrn2_recurrence(heads(q_c, HG_HEADS), heads(k_in, HG_HEADS),
                             heads(hg_i.astype(f32), HG_HEADS), heads(log_f, HG_HEADS))
    o_hg = (_rms_norm(o_hg, hg_gain) * jax.nn.silu(heads(hg_g, HG_HEADS).astype(f32)))
    o_hg = o_hg.reshape(bsz, seq, HG_WV)

    o = jnp.concatenate([o_sb.astype(f32), o_gd, o_hg], axis=-1).astype(h.dtype)
    return o @ w_out

def setup_inputs(seed: int = 0) -> dict:
    key = jax.random.key(seed)
    ks = jax.random.split(key, 24)

    def nrm(k, shape, scale):
        return jax.random.normal(k, shape, jnp.float32) * scale

    def gain(k, shape):
        return 1.0 + nrm(k, shape, 0.02)

    dt = jnp.exp(jax.random.uniform(ks[10], (DEPTH, GDN_HEADS), jnp.float32,
                                    minval=math.log(1e-3), maxval=math.log(1e-1)))
    return {
        'x': nrm(ks[0], (BATCH, SEQ, D_MODEL), 1.0),
        'c': nrm(ks[1], (BATCH, D_MODEL), 1.0),
        'ffn1_norm': gain(ks[2], (DEPTH, D_MODEL)),
        'ffn1_w_in': nrm(ks[3], (DEPTH, D_MODEL, 2 * D_FF), D_MODEL ** -0.5),
        'ffn1_w_out': nrm(ks[4], (DEPTH, D_FF, D_MODEL), D_FF ** -0.5),
        'mix_norm': gain(ks[5], (DEPTH, D_MODEL)),
        'mix_w_in': nrm(ks[6], (DEPTH, D_MODEL, D_IN), D_MODEL ** -0.5),
        'gdn_conv_w': nrm(ks[7], (DEPTH, GDN_CONV, GDN_WK * 2 + GDN_WV), GDN_CONV ** -0.5),
        'gdn_A_log': jnp.log(jax.random.uniform(ks[8], (DEPTH, GDN_HEADS), jnp.float32,
                                                minval=1.0, maxval=16.0)),
        'gdn_dt_bias': dt + jnp.log(-jnp.expm1(-dt)),
        'sb_out_norm': gain(ks[11], (DEPTH, SB_DIM)),
        'gdn_out_norm': gain(ks[12], (DEPTH, GDN_DV)),
        'hg_out_norm': gain(ks[13], (DEPTH, HG_DV)),
        'hg_lb_logits': nrm(ks[14], (DEPTH, HG_WK), 0.1),
        'mix_w_out': nrm(ks[15], (DEPTH, D_MIX, D_MODEL), D_MIX ** -0.5),
        'ffn2_norm': gain(ks[16], (DEPTH, D_MODEL)),
        'ffn2_w_in': nrm(ks[17], (DEPTH, D_MODEL, 2 * D_FF), D_MODEL ** -0.5),
        'ffn2_w_out': nrm(ks[18], (DEPTH, D_FF, D_MODEL), D_FF ** -0.5),
        'ada_w': nrm(ks[19], (DEPTH, D_MODEL, N_MOD * D_MODEL), 0.5 * D_MODEL ** -0.5),
        'ada_b': nrm(ks[20], (DEPTH, N_MOD * D_MODEL), 0.01),
        'final_norm': gain(ks[21], (D_MODEL,)),
    }

def reference(x, c, ffn1_norm, ffn1_w_in, ffn1_w_out, mix_norm, mix_w_in, gdn_conv_w,
              gdn_A_log, gdn_dt_bias, sb_out_norm, gdn_out_norm, hg_out_norm, hg_lb_logits,
              mix_w_out, ffn2_norm, ffn2_w_in, ffn2_w_out, ada_w, ada_b, final_norm):
    lb_cum = jnp.cumsum(jax.nn.softmax(hg_lb_logits.astype(jnp.float32), axis=0), axis=0)
    lower_bounds = lb_cum - lb_cum[0:1]
    c_act = jax.nn.silu(c)
    bsz = x.shape[0]
    for layer in range(DEPTH):
        mod = (c_act @ ada_w[layer] + ada_b[layer]).reshape(bsz, N_MOD, D_MODEL)
        m = [mod[:, i] for i in range(N_MOD)]
        h = _modulate(_rms_norm(x, ffn1_norm[layer]), m[0], m[1])
        x = x + HALF_STEP * m[2][:, None, :] * _swiglu(h, ffn1_w_in[layer], ffn1_w_out[layer])
        h = _modulate(_rms_norm(x, mix_norm[layer]), m[3], m[4])
        y = _hybrid_mixer(h, mix_w_in[layer], gdn_conv_w[layer], gdn_A_log[layer],
                          gdn_dt_bias[layer], sb_out_norm[layer], gdn_out_norm[layer],
                          hg_out_norm[layer], lower_bounds[layer], mix_w_out[layer])
        x = x + m[5][:, None, :] * y
        h = _modulate(_rms_norm(x, ffn2_norm[layer]), m[6], m[7])
        x = x + HALF_STEP * m[8][:, None, :] * _swiglu(h, ffn2_w_in[layer], ffn2_w_out[layer])
    return _rms_norm(x, final_norm)


_drawn_inputs = setup_inputs


def setup_inputs(seed=0):
    import zlib

    import numpy as np

    out = dict(_drawn_inputs(seed))
    spreads = {}
    factors = {'ffn1_norm': 8.0,
     'mix_norm': 6.227,
     'sb_out_norm': 181.977,
     'gdn_out_norm': 33.504,
     'hg_out_norm': 27.663,
     'hg_lb_logits': 8.0,
     'ffn2_norm': 25.947,
     'ada_b': 3.798,
     'final_norm': 21.075}
    for name, (base, spread) in spreads.items():
        noise = np.random.default_rng([zlib.crc32(name.encode()), seed]).standard_normal(out[name].shape)
        drawn = base * np.exp(spread * noise) if base else spread * noise
        out[name] = __import__('jax').numpy.asarray(drawn.astype(out[name].dtype))
    for name, factor in factors.items():
        out[name] = (out[name] * factor).astype(out[name].dtype)
    return out
```

```python
from contextlib import ExitStack

import numpy as np

import concourse.bass as bass
from concourse import mybir

ALU = mybir.AluOpType
ACT = mybir.ActivationFunctionType
F32 = mybir.dt.float32
F32R = mybir.dt.float32r
I32 = mybir.dt.int32

P = 128
DEPTH = 2
T = 512
NT = T // P
DM = 1024
KT = DM // P
FF = 2816
FT = FF // P
EPS = 1e-6
HEADS = 4

W8 = KT * P
HALF_FT = FT // 2
W11 = HALF_FT * P
RAW = 4
FEAT_UNITS = 24
TOK_A, TOK_B = 512, 264
ADA_GROUPS = 18

U_IN1, U_OUT1, U_MIX, U_MOUT, U_IN2, U_OUT2, U_ALL = 0, 44, 60, 92, 100, 144, 160
R_IN1, R_OUT1, R_MIX, R_MOUT, R_IN2, R_OUT2, R_ALL = 0, 84, 116, 148, 156, 200, 232
UNIT_AT, ADA_AT = (0, 3, 6, 7), (1, 2, 4, 5)

GK, GQ, GV, GZ, HQ, HG, SQ, SK = 0, 4, 8, 12, 16, 18, 20, 22
C_ONES, C_BD, C_ID, C_U, C_NU, C_NONES, C_POSA, C_NEGD, C_STRICT, C_SNEG = range(10)
C_M = 10
C_MT = 17
L2_AT = 5
C_PICK = 24
NC = 25
LEVELS = 7
BIG = 1.0e30

Q_GAIN, Q_ADAB, Q_CONV, Q_SB, Q_GD, Q_HG, Q_AL, Q_DT, Q_FL, Q_NEG = 0, 24, 96, 144, 145, 146, 147, 151, 155, 156
NQ = 157
SB_OFF = (0, 512, 896, 1152)
SB_BANK = ((0, 0), (1, 0), (2, 0), (2, 256))
SB_W = 1280
FIN_TILE = (0, 1, 6, 7, 2, 3, 4, 5)
Z_BANK = (0, 1, 6, 7)

PER_LAYER = dict(
    raw_used=232, hi_done=160, unit_done=160, ada_sum=18, ada_step=72, mod_step=18, silu_done=44, gated=44,
    act_h=44, act_split=44, x_add=24, sq_step=21, sq_done=24, ms_sum=3, rs_done=3, norm_t=24, norm_hi=24,
    norm_lo=24, evac=24, conv_v=12, conv_silu=12, tok_copied=4, v_step=195, s_step=45, p_step=6, bar=6, sb_z=4,
    sb_zs=4, sb_sp=4, sb_cum=4, sb_lw=4, sb_ln=4, sb_w=4, sb_o=4, fin_sq=8, fin_sum=8, fin_rs=8, fin_y=8,
    fin_hi=8, fin_lo=8, lb_v=1, lb_s=1, hg_v=3, hg_s=3, hg_logf=1, hg_sums=1, hg_turned=1, hg_ktok=1, hg_btok=2,
    hg_bfeat=1, hg_kdec=1, hg_kT=1, hg_ds=1, hg_ds_read=1, hg_state=1, hg_qe=1, hg_zero=1, hl_prod=1, hl_diag=1,
    hl_arg=7, hl_low=7, hl_exp=7, hl_k=7, hl_h=7, hl_gram=7, hl_put=7, ho_done=2, gd_v=3, gd_s=3, gd_la=1,
    gd_cum=1, gd_cols=1, gd_sq=8, gd_row=8, gd_rows=1, gd_l2x=8, gd_rs=1, gd_l2=8, gc_bc=4, gc_row=4, gc_arg=4,
    gc_exp=4, gc_pairs=4, gc_turned=4, gc_a=4, gc_q=4, gc_kv=4, gi_mask=28, gi_z=28, gi_zc=24, gi_xy=24,
    gi_up=28, gw_mm=4, gw_copied=4, gs_v=4, gs_vn=4, gs_ds=3, gs_state=12, gs_o=4,
)


def constants():
    c = np.zeros((NC, P, P), np.float32)
    i = np.arange(P)
    row, col = i[:, None], i[None, :]
    c[C_ONES] = 1
    c[C_BD] = row // 64 == col // 64
    c[C_ID] = row == col
    c[C_U] = row <= col
    c[C_NU] = -(row >= col).astype(np.float32)
    c[C_NONES] = -1
    c[C_POSA] = np.where(col < row, 0, BIG)
    c[C_NEGD] = np.where(col >= row, 0, -BIG)
    c[C_STRICT] = row < col
    c[C_SNEG] = np.where(row < col, 0, -BIG)
    c[C_PICK][:, 7] = 1
    for level in range(LEVELS):
        b = 1 << level
        m = (row // (2 * b) == col // (2 * b)) & (row // b % 2 == 1) & (col // b % 2 == 0)
        c[C_M + level] = m
        c[C_MT + level] = m.T
    return np.ascontiguousarray(c.transpose(1, 0, 2))


class Stage:

    def __init__(self, nc, ctx, name, n, free=0):
        self.sem, self.name, self.n, self.free, self.seen = ctx.enter_context(nc.semaphore(name)), name, n, free, 0

    def step(self, times=1):
        self.seen += times
        return self.sem

    def after(self, layer, k, i=0, per=0):
        return layer * self.n + i * per + (self.free + k)

    def now(self, layer):
        return self.after(layer, self.seen)

    def freed(self, layer, k, i=0, per=0):
        return layer * self.n + i * per + (k + 1)


def build(nc, x, c, prm, consts, lb_logits, final_gain, ada_w, ffn_in, ffn_out, mix_feat, mix_ta, mix_tb, mix_out, out):
    with ExitStack() as ctx:
        def sb(name, shape, dt=F32, on=ctx):
            return on.enter_context(nc.sbuf_tensor(name, shape, dt))

        used = []

        def stage(name, free=0):
            used.append(Stage(nc, ctx, name, PER_LAYER.get(name, 0), free))
            return used[-1]

        X = sb("X", [P, KT, T])
        with ExitStack() as region:
            h_hi = sb("h_hi", [P, KT, T], F32R, region)
            h_lo = sb("h_lo", [P, KT, T], F32R, region)
        HX = sb("HX", [P, 2 * KT * T])
        with ExitStack() as region:
            act_hi = sb("act_hi", [P, FT, T], F32R, region)
            act_lo = sb("act_lo", [P, FT, T], F32R, region)
        M = sb("M", [P, 2 * FT * T])
        raw = [sb(f"raw{s}", [P, W11]) for s in range(RAW)]
        w_hi, w_lo = [sb("w_hi0", [P, W11], F32R)], [sb("w_lo0", [P, W11], F32R)]
        with ExitStack() as region:
            w_hi.append(sb("w_hi1", [P, W11], F32R, region))
            w_lo.append(sb("w_lo1", [P, W11], F32R, region))
        W1 = sb("W1", [P, 2 * W11])
        ones = sb("ones", [P, P])
        PRM = sb("PRM", [P, DEPTH, NQ])
        cur = sb("cur", [P, NQ])
        c_act = sb("c_act", [P, 2, KT])
        fin_gain = sb("fin_gain", [P, KT])
        mods = sb("mods", [P, 72])
        mods_next = sb("mods_next", [P, 16])
        gate_c = sb("gate_c", [P, 2, KT])
        mod_a = sb("mod_a", [P, KT])
        ada_acc = sb("ada_acc", [P, 512])
        tmpA = sb("tmpA", [P, 2, T])
        tmpB = sb("tmpB", [P, 2, T])
        sumsq = sb("sumsq", [P, T])
        squares = sb("squares", [P, T])
        padded = sb("padded", [P, 2, T + 3])

        PRO = [M[:, g * 4096:(g + 1) * 4096].rearrange("p (k e) -> p k e", k=4) for g in range(4)]
        big = M[:, 0:FEAT_UNITS * T].rearrange("p (t n) -> p t n", n=T)
        o = FEAT_UNITS * T
        TFI = M[:, o:o + 2048].rearrange("p (a n e) -> p a n e", a=2, n=NT)
        TF, TI, TV, spare = (M[:, o + 1024 * a:o + 1024 * (a + 1)] for a in range(4))
        TFTI, TVS = M[:, o:o + 2048], M[:, o + 2048:o + 4096]
        o += 4096
        MC = M[:, o:o + NC * P].rearrange("p (c n) -> p c n", c=NC)
        o += NC * P
        LB = M[:, o:o + 512].rearrange("p (a e) -> p a e", a=2)
        lb_in = M[:, o + 768:o + 1280]
        lb_t = M[:, o + 512:o + 768]
        lb_d = M[:, o + 1280:o + 1536]
        KC_PLACE = M[:, o:o + 2048]
        HAT = M[:, o + 768:o + 2816].rearrange("p (h t) -> p h t", h=HEADS)
        tiles = lambda t, n: M[:, t * T:(t + n) * T]
        Z = [W1[:, W11 * b:W11 * b + SB_W] for b in range(2)]
        SP = [HX[:, 5120 + SB_W * b:5120 + SB_W * (b + 1)] for b in range(2)]
        HQT, HE, HE1, HLS, HLF, HK = tiles(HQ, 2), HX[:, 1024:2048], HX[:, 5120:6144], HX[:, 2048:3072], HX[:, 3072:4096], TF
        HB, HKT, HQE, HKD = tiles(SQ, 2), tiles(SK, 2), TV, HLS
        H, HEXP = [HLF, spare], [HE, HE1]
        HQ2 = [HX[:, a:a + 1024].rearrange("p (c h e) -> p c h e", c=8, h=2) for a in (6144, 7168)]
        HPROD = tmpB[:, :, :].rearrange("p a t -> p (a t)")
        HS = HK.rearrange("p (a n e) -> p a n e", a=2, n=NT)
        v4 = lambda a: a.rearrange("p (n h e) -> p n h e", n=NT, h=HEADS)
        GA, GAM, GX, GY, GT, GAQ, GKC = (v4(a) for a in (
            HX[:, 1024:3072], HX[:, 5120:7168], tiles(SQ, 4), tiles(HQ, 4), TFTI, TVS, KC_PLACE))
        smalls = sb("smalls", [P, 480])
        at = [0]

        def small(n):
            at[0] += n
            return smalls[:, at[0] - n:at[0]]

        BA, G_X, G_E, G_LS = small(32), small(32), small(32), small(32)
        G_LA, G_BETA, G_G, G_TOT, G_TG, G_EG, G_EKD, G_CD, G_CB = (small(16) for _ in range(9))
        G_EA, H_CD = small(4), small(8)
        cols = lambda a, level, half: a.rearrange("p (m s w) -> p m s w", s=2, w=1 << level)[:, :, half, :]
        nh = lambda a, n: a[:, 4 * n:4 * n + 4].unsqueeze(2).to_broadcast([P, HEADS, P])

        banks = [ctx.enter_context(nc.psum_tensor(f"bank{b}", [P, 512], F32))[:, :] for b in range(8)]
        flat = lambda a: a.rearrange("p h e -> p (h e)")

        def sem(name):
            return ctx.enter_context(nc.semaphore(name))

        small_loaded, x_loaded, mixer_constants, out_written = sem("small_loaded"), sem("x_loaded"), sem("mixer_constants"), sem("out_written")
        raw_loaded = [sem(f"raw_loaded{s}") for s in range(RAW)]
        pro_loaded = [sem(f"pro_loaded{k}") for k in range(8)]
        pro_ones, pro_act, pro_sum, pro_mod, pro_v, pro_sq = (sem(n) for n in (
            "pro_ones", "pro_act", "pro_sum", "pro_mod", "pro_v", "pro_sq"))
        final_sum, final_rs, final_done = sem("final_sum"), sem("final_rs"), sem("final_done")
        raw_used = stage("raw_used", RAW)
        hi_done = stage("hi_done")
        unit_done = stage("unit_done", 2)
        ada_sum, ada_step, mod_step = stage("ada_sum"), stage("ada_step"), stage("mod_step", 1)
        silu_done, gated = stage("silu_done"), stage("gated", 2)
        act_h, act_split = stage("act_h"), stage("act_split", 2)
        x_add, sq_step, sq_done = stage("x_add", 2), stage("sq_step"), stage("sq_done", 8)
        ms_sum, rs_done = stage("ms_sum"), stage("rs_done")
        norm_t, norm_hi, norm_lo = stage("norm_t"), stage("norm_hi"), stage("norm_lo", 2)
        evac, conv_v, conv_silu = stage("evac"), stage("conv_v", 2), stage("conv_silu", 2)
        tok_copied = stage("tok_copied")
        v_step, s_step, p_step = stage("v_step"), stage("s_step"), stage("p_step")
        bar = stage("bar")
        sb_z, sb_zs, sb_sp, sb_cum, sb_lw, sb_ln, sb_w, sb_o = (stage(n) for n in (
            "sb_z", "sb_zs", "sb_sp", "sb_cum", "sb_lw", "sb_ln", "sb_w", "sb_o"))
        fin_sq, fin_sum, fin_rs, fin_y, fin_hi, fin_lo = (stage(n) for n in (
            "fin_sq", "fin_sum", "fin_rs", "fin_y", "fin_hi", "fin_lo"))
        lb_v, lb_s, hg_v, hg_s = stage("lb_v"), stage("lb_s"), stage("hg_v"), stage("hg_s")
        hg_logf, hg_sums, hg_turned, hg_ktok, hg_btok, hg_bfeat, hg_kdec, hg_kT, hg_ds, hg_ds_read, hg_state, hg_qe = (stage(n) for n in (
            "hg_logf", "hg_sums", "hg_turned", "hg_ktok", "hg_btok", "hg_bfeat", "hg_kdec", "hg_kT", "hg_ds", "hg_ds_read", "hg_state", "hg_qe"))
        hg_zero, hl_prod, hl_diag, hl_arg, hl_low, hl_exp, hl_k, hl_h, hl_gram, hl_put, ho_done = (stage(n) for n in (
            "hg_zero", "hl_prod", "hl_diag", "hl_arg", "hl_low", "hl_exp", "hl_k", "hl_h", "hl_gram", "hl_put", "ho_done"))
        gd_v, gd_s, gd_la, gd_cum, gd_cols, gd_sq, gd_row, gd_rows, gd_l2x, gd_rs, gd_l2 = (stage(n) for n in (
            "gd_v", "gd_s", "gd_la", "gd_cum", "gd_cols", "gd_sq", "gd_row", "gd_rows", "gd_l2x", "gd_rs", "gd_l2"))
        gc_bc, gc_row, gc_arg, gc_exp, gc_pairs, gc_turned, gc_a, gc_q, gc_kv = (stage(n) for n in (
            "gc_bc", "gc_row", "gc_arg", "gc_exp", "gc_pairs", "gc_turned", "gc_a", "gc_q", "gc_kv"))
        gi_mask, gi_z, gi_zc, gi_xy, gi_up = (stage(n) for n in ("gi_mask", "gi_z", "gi_zc", "gi_xy", "gi_up"))
        gw_mm, gw_copied = stage("gw_mm"), stage("gw_copied")
        gs_v, gs_vn, gs_ds, gs_state, gs_o = (stage(n) for n in ("gs_v", "gs_vn", "gs_ds", "gs_state", "gs_o"))

        def wait_raw(eng, layer, r, i=0, per=0):
            eng.wait_ge(raw_loaded[r % RAW], (layer * (R_ALL // RAW) + i * (per // RAW) + (r // RAW + 1)) * 16)

        def barrier(eng, layer, k):
            eng.drain().then_inc(bar.step(), 1)
            eng.wait_ge(bar.sem, bar.after(layer, 3 * (k + 1)))

        FFNS = ((0, U_IN1, U_OUT1, R_IN1, R_OUT1, True, 10), (1, U_IN2, U_OUT2, R_IN2, R_OUT2, False, 14))
        PLAIN = (0, 1, 2, 3)
        block = ctx.enter_context(nc.Block())

        @block.sync
        def _(sp):
            sp.dma_start(c_act[:, 0, :], c).then_inc(small_loaded, 16)
            sp.dma_start(PRM[:, :, :], prm).then_inc(small_loaded, 16)
            sp.dma_start(fin_gain[:, :], final_gain).then_inc(small_loaded, 16)
            for k in range(8):
                sp.dma_start(PRO[k // 2][:, k % 2 * 2:k % 2 * 2 + 2, :], ada_w[DEPTH - 1, 14 + k // 2, k % 2 * 2:k % 2 * 2 + 2].rearrange(
                    "k p e -> p k e")).then_inc(pro_loaded[k], 16)
                if k < 2:
                    sp.dma_start(X[:, 4 * k:4 * k + 4, :], x[:, 4 * k:4 * k + 4, :]).then_inc(x_loaded, 16)

            def load(layer, r, src, i=0, per=0):
                s = r % RAW
                sp.wait_ge(raw_used.sem, raw_used.freed(layer, r, i, per))
                sp.dma_start(raw[s][:, 0:src.shape[-1]], src).then_inc(raw_loaded[s], 16)

            def step(layer, r, units, pieces, i=0):
                order, per = (UNIT_AT, 8) if pieces else (PLAIN, 4)
                for k in range(4):
                    load(layer, r + order[k], units(k), i, per)
                    if pieces and k < 2:
                        for kk in (2 * k, 2 * k + 1):
                            load(layer, r + ADA_AT[kk], pieces(kk), i, per)

            with sp.Fori(0, DEPTH) as layer:
                for f, _, _, r_in, r_out, ada, g in FFNS:
                    if f == 1:
                        for u in range(FEAT_UNITS):
                            load(layer, R_MIX + u, mix_feat[layer, u])
                            if u == 4:
                                sp.wait_ge(ms_sum.sem, ms_sum.after(layer, 2))
                                sp.dma_start(MC, consts).then_inc(mixer_constants, 16)
                                sp.dma_start(lb_in, lb_logits).then_inc(mixer_constants, 16)
                        for u in range(4):
                            load(layer, R_MIX + FEAT_UNITS + u, mix_ta[layer, u])
                        for u in range(4):
                            load(layer, R_MIX + FEAT_UNITS + 4 + u, mix_tb[layer, u])
                        for u in range(KT):
                            load(layer, R_MOUT + u, mix_out[layer, u])
                    with sp.Fori(0, 10) as i:
                        step(layer, r_in, lambda k: ffn_in[layer, f, i * 4 + k], (lambda kk: ada_w[layer, i, kk]) if ada else None, i)
                    step(layer, r_in + (80 if ada else 40), lambda k: ffn_in[layer, f, 40 + k], None)
                    with sp.Fori(0, 4) as i:
                        step(layer, r_out, lambda k: ffn_out[layer, f, i * 4 + k], lambda kk: ada_w[layer, i + g, kk], i)
            sp.wait_ge(final_done, KT)
            sp.dma_start(out, X[:, :, :]).then_inc(out_written, 16)
            sp.wait_ge(out_written, 16)

        @block.tensor
        def _(pe):
            mc = lambda a: MC[:, a, :]

            def split_ready(layer, r, i=0, per=0):
                pe.wait_ge(raw_used.sem, raw_used.after(layer, r + 1, i, per))

            def unit(u, count, dst, m_hi, m_lo, start=True, stop=True, before=None, times=1):
                for k in range(count):
                    if before is not None:
                        before(k)
                    hi, lo = (w[u % 2][:, k * P:(k + 1) * P] for w in (w_hi, w_lo))
                    pe.matmul(dst, hi, m_hi(k), start=start and k == 0, stop=False)
                    pe.matmul(dst, hi, m_lo(k), start=False, stop=False)
                    last = pe.matmul(dst, lo, m_hi(k), start=False, stop=stop and k == count - 1)
                last.then_inc(unit_done.step(times), 1)

            def ada_columns():
                for a in range(4):
                    last = pe.matmul(banks[7][:, a:a + 1], ada_acc[:, a * P:(a + 1) * P], ones[:, 0:1], start=True, stop=True)
                return last

            def norm_sum(layer, n):
                pe.wait_ge(sq_done.sem, sq_done.after(layer, 8 * n))
                pe.matmul(banks[6][:, :], ones[:, :], sumsq[:, :], start=True, stop=True).then_inc(ms_sum.step(), 1)

            H_HI, H_LO = (lambda k: h_hi[:, k, :]), (lambda k: h_lo[:, k, :])

            def step_in(layer, f, r, chunk, ada, i=0, times=1, first=False):
                order, per = (UNIT_AT, 8) if ada else (PLAIN, 4)
                for k in range(4):
                    split_ready(layer, r + order[k], i, per)
                    if k % 2 == 0:
                        pe.wait_ge(gated.sem, gated.freed(layer, 22 * f + chunk + k // 2, i, 2))
                    unit(k, KT, banks[k], H_HI, H_LO, times=times,
                         before=(lambda kk: pe.wait_ge(norm_lo.sem, norm_lo.after(layer, 16 * f + kk + 1))) if first and k == 0 else None)
                    if ada and k == 2:
                        split_ready(layer, r + ADA_AT[3], i, per)
                        ada_columns().then_inc(ada_sum.step(times), 1)

            def step_out(layer, f, r, m, i=0, times=1, first=False):
                for k in range(4):
                    b = k % 2 * HALF_FT
                    split_ready(layer, r + UNIT_AT[k], i, 8)
                    if k % 2 == 0:
                        pe.wait_ge(x_add.sem, x_add.freed(layer, 16 * f + m + k // 2, i, 2))
                    unit(k, HALF_FT, banks[4 + k // 2], lambda j, b=b: act_hi[:, b + j, :], lambda j, b=b: act_lo[:, b + j, :],
                         start=k % 2 == 0, stop=k % 2 == 1, times=times,
                         before=(lambda j, b=b: pe.wait_ge(act_split.sem, act_split.after(layer, 22 * f + b + j + 1))) if first and k < 2 else None)
                    if k == 2:
                        split_ready(layer, r + ADA_AT[3], i, 8)
                        ada_columns().then_inc(ada_sum.step(times), 1)

            def finish(k, mat, bank):
                pe.wait_ge(fin_sq.sem, fin_sq.after(layer, k + 1))
                pe.matmul(bank, mat, tmpB[:, k % 2, :], start=True, stop=True).then_inc(fin_sum.step(), 1)

            pe.wait_ge(pro_ones, 1)
            for g in range(4):
                pe.wait_ge(pro_v, 8 * (g + 1))
                if g:
                    pe.wait_ge(pro_mod, g)
                ada_columns().then_inc(pro_sum, 1)

            with pe.Fori(0, DEPTH) as layer:
                for f, _, _, r_in, r_out, ada, _ in FFNS:
                    if f == 1:
                        norm_sum(layer, 1)
                        for u in range(FEAT_UNITS):
                            split_ready(layer, R_MIX + u)
                            if u >= 2:
                                pe.wait_ge(evac.sem, evac.after(layer, u - 1))
                            if L2_AT <= u < L2_AT + 8:
                                t = u - L2_AT
                                if t == 0:
                                    pe.wait_ge(mixer_constants, layer * 32 + 32)
                                pe.wait_ge(gd_sq.sem, gd_sq.after(layer, t + 1))
                                pe.matmul(banks[6][0:8, :], MC[:, C_PICK, 7 - t:15 - t], tmpA[:, t % 2, :],
                                          start=t == 0, stop=t == 7, skip_group_check=True).then_inc(gd_row.step(), 1)
                            unit(u, KT, banks[u % 2], H_HI, H_LO,
                                 before=(lambda kk: pe.wait_ge(norm_lo.sem, norm_lo.after(layer, 8 + kk + 1))) if u == 0 else None)
                        for ab, width in ((0, TOK_A), (1, TOK_B)):
                            for kp in range(4):
                                u = FEAT_UNITS + 4 * ab + kp
                                split_ready(layer, R_MIX + u)
                                if ab == 1 and kp == 0:
                                    pe.wait_ge(gd_rows.sem, gd_rows.after(layer, 1))
                                    pe.wait_ge(evac.sem, evac.after(layer, FEAT_UNITS))
                                for n in range(NT):
                                    dst = banks[(2 + 4 * ab + n) % 8][:, 0:width]
                                    for k2 in range(2):
                                        k = 2 * kp + k2
                                        wh, wl = (w[u % 2][:, k2 * width:(k2 + 1) * width] for w in (w_hi, w_lo))
                                        th, tl = (h[:, k, n * P:(n + 1) * P] for h in (h_hi, h_lo))
                                        pe.matmul(dst, th, wh, start=k == 0, stop=False)
                                        pe.matmul(dst, tl, wh, start=False, stop=False)
                                        last = pe.matmul(dst, th, wl, start=False, stop=k == KT - 1)
                                last.then_inc(unit_done.step(), 1)
                        barrier(pe, layer, 0)

                        pe.wait_ge(mixer_constants, layer * 32 + 32)

                        def scores(h):
                            p0, b0 = 64 * (h % 2), 3 * (h % 2)
                            q, k = big[p0:p0 + 64, SQ + h // 2, :], big[p0:p0 + 64, SK + h // 2, :]
                            if h >= 2:
                                pe.wait_ge(sb_lw.sem, sb_lw.after(layer, h - 1))
                            for kb in range(NT):
                                b, c0 = SB_BANK[kb]
                                last = pe.matmul(banks[b0 + b][:, c0:c0 + T - kb * P], k[:, kb * P:(kb + 1) * P], q[:, kb * P:T],
                                                 start=True, stop=True)
                            last.then_inc(sb_z.step(), 1)

                        def sums(h):
                            pe.wait_ge(sb_sp.sem, sb_sp.after(layer, h + 1))
                            for kb in range(NT):
                                for jb in range(kb, NT):
                                    w = T - jb * P
                                    b, c0 = SB_BANK[kb]
                                    c0 += (jb - kb) * P
                                    last = pe.matmul(banks[3 * (h % 2) + b][:, c0:c0 + w], mc(C_NU if jb == kb else C_NONES),
                                                     SP[h % 2][:, SB_OFF[jb]:SB_OFF[jb] + w], start=jb == kb, stop=jb == NT - 1,
                                                     skip_group_check=True)
                            last.then_inc(sb_cum.step(), 1)

                        def outputs(h):
                            p0 = 64 * (h % 2)
                            pe.wait_ge(sb_w.sem, sb_w.after(layer, h + 1))
                            for kb in range(NT):
                                last = pe.matmul(banks[6 + h // 2][p0:p0 + 64, kb * P:T], TV[:, kb * 256 + h * 64:kb * 256 + (h + 1) * 64],
                                                 SP[h % 2][:, SB_OFF[kb]:SB_OFF[kb] + T - kb * P], start=kb == 0, stop=kb == NT - 1,
                                                 skip_group_check=True)
                            last.then_inc(sb_o.step(), 1)

                        scores(0)
                        scores(1)
                        sums(0)
                        sums(1)
                        scores(2)
                        outputs(0)
                        scores(3)
                        outputs(1)
                        sums(2)
                        sums(3)
                        finish(0, mc(C_BD), banks[6])
                        outputs(2)
                        outputs(3)

                        pe.wait_ge(hg_logf.sem, hg_logf.after(layer, 1))
                        pe.wait_ge(sb_lw.sem, sb_lw.after(layer, HEADS))
                        for n in range(NT):
                            lf = HLF[:, n * 256:(n + 1) * 256]
                            a = n % 2 * 256
                            pe.matmul(banks[n // 2][:, a:a + 256], mc(C_U), lf, start=True, stop=True)
                            pe.matmul(banks[2 + n // 2][:, a:a + 256], mc(C_ONES), lf, start=True, stop=True)
                            for pr in range(2):
                                last = pe.matmul(banks[4 + pr][:, n * P:(n + 1) * P], lf[:, pr * P:(pr + 1) * P], mc(C_U), start=True, stop=True)
                        last.then_inc(hg_sums.step(), 1)
                        finish(1, mc(C_BD), banks[7])
                        pe.wait_ge(hg_ktok.sem, hg_ktok.after(layer, 1))
                        pe.wait_ge(fin_rs.sem, fin_rs.after(layer, 2))
                        for n in range(NT):
                            for pr in range(2):
                                last = pe.transpose(banks[6 + pr][:, n * P:(n + 1) * P],
                                                    HK[:, n * 256 + pr * P:n * 256 + (pr + 1) * P], mc(C_ID))
                        last.then_inc(hg_turned.step(), 1)
                        pe.wait_ge(hg_kdec.sem, hg_kdec.after(layer, 1))
                        pe.wait_ge(hg_bfeat.sem, hg_bfeat.after(layer, 1))
                        for n in range(NT):
                            for pr in range(2):
                                a = n * 256 + pr * P
                                last = pe.matmul(banks[4 + pr][:, n * P:(n + 1) * P], HKD[:, a:a + P], TI[:, a:a + P], start=True, stop=True)
                        last.then_inc(hg_ds.step(), 1)

                        pe.wait_ge(hl_prod.sem, hl_prod.after(layer, 1))
                        for c in range(8):
                            last = pe.matmul(banks[7][:, 2 * c:2 * c + 2], HPROD[:, c * P:(c + 1) * P], MC[:, C_BD, 0:P:64], start=True, stop=True)
                        last.then_inc(hl_diag.step(), 1)
                        pe.wait_ge(hg_zero.sem, hg_zero.after(layer, 1))
                        for level in range(LEVELS):
                            b = level % 2
                            pe.wait_ge(hl_k.sem, hl_k.after(layer, level + 1))
                            pe.wait_ge(hl_h.sem, hl_h.after(layer, level + 1))
                            if level >= 2:
                                pe.wait_ge(hl_put.sem, hl_put.after(layer, level - 1))
                            for c in range(8):
                                last = pe.matmul(banks[2 * b + c // NT][:, c % NT * P:(c % NT + 1) * P], H[b][:, c * P:(c + 1) * P],
                                                 HQ2[b][:, c, :, :], start=True, stop=True)
                            last.then_inc(hl_gram.step(), 1)
                        pe.wait_ge(hg_state.sem, hg_state.after(layer, 1))
                        pe.wait_ge(hg_qe.sem, hg_qe.after(layer, 1))
                        pe.wait_ge(hl_put.sem, hl_put.after(layer, LEVELS))
                        for pr in range(2):
                            for n in range(NT):
                                a = slice(n * P, (n + 1) * P)
                                if n:
                                    pe.matmul(banks[6 + pr][:, a], HS[:, pr, n, :], HQE[:, pr * T + n * P:pr * T + (n + 1) * P],
                                              start=True, stop=False, skip_group_check=True)
                                for hh in range(2):
                                    h = 2 * pr + hh
                                    last = pe.matmul(banks[6 + pr][64 * hh:64 * hh + 64, a], TI[:, n * 256 + h * 64:n * 256 + (h + 1) * 64],
                                                     HAT[:, h, a], start=n == 0, stop=True, skip_group_check=True)
                            last.then_inc(ho_done.step(), 1)
                        barrier(pe, layer, 1)

                        pe.wait_ge(gd_la.sem, gd_la.after(layer, 1))
                        pe.matmul(banks[0][:, 0:16], mc(C_U), G_LA, start=True, stop=True)
                        pe.matmul(banks[1][:, 0:16], mc(C_ONES), G_LA, start=True, stop=True).then_inc(gd_cum.step(), 1)
                        for k in range(2):
                            finish(2 + k, mc(C_BD), banks[4 + k])

                        def decay_rows(n):
                            b = n % 2
                            pe.wait_ge(gc_bc.sem, gc_bc.after(layer, n + 1))
                            if n >= 2:
                                pe.wait_ge(gc_exp.sem, gc_exp.after(layer, n - 1))
                            for h in range(HEADS):
                                last = pe.matmul(banks[b][:, h * P:(h + 1) * P], GX[:, b, h, :], mc(C_U), start=True, stop=True)
                            last.then_inc(gc_row.step(), 1)

                        def pairs(n):
                            a, b = slice(n * P, (n + 1) * P), n % 2
                            if n >= 2:
                                pe.wait_ge(gc_kv.sem, gc_kv.after(layer, n - 1))
                            for h in range(HEADS):
                                kk, c0 = big[:, GK + h, a], slice(h * P, (h + 1) * P)
                                pe.matmul(banks[2 + b][:, c0], kk, kk, start=True, stop=True)
                                pe.matmul(banks[4 + b][:, c0], kk, big[:, GQ + h, a], start=True, stop=True)
                            if n:
                                pe.wait_ge(gc_turned.sem, gc_turned.after(layer, n))
                            for h in range(HEADS):
                                c0 = slice(h * P, (h + 1) * P)
                                pe.transpose(banks[6][:, c0], big[:, GK + h, a], mc(C_ID))
                                last = pe.transpose(banks[7][:, c0], big[:, GV + h, a], mc(C_ID))
                            last.then_inc(gc_pairs.step(), 1)

                        pe.wait_ge(gd_rs.sem, gd_rs.after(layer, 1))
                        for t in range(8):
                            if t >= 2:
                                pe.wait_ge(gd_l2.sem, gd_l2.after(layer, t - 1))
                            pe.matmul(banks[2 + t % 2], MC[0:8, C_ID, t:t + 1].to_broadcast([8, P]), squares[0:8, :],
                                      start=True, stop=True).then_inc(gd_l2x.step(), 1)
                            if t in (3, 5):
                                decay_rows((t - 3) // 2)
                        pe.wait_ge(gd_l2.sem, gd_l2.after(layer, 8))
                        pe.wait_ge(gd_cols.sem, gd_cols.after(layer, 1))
                        pe.wait_ge(fin_y.sem, fin_y.after(layer, 4))
                        for n in range(NT):
                            pairs(n)
                            if n < NT - 2:
                                decay_rows(n + 2)
                        pe.wait_ge(gc_kv.sem, gc_kv.after(layer, NT))
                        for level in range(LEVELS):
                            for n in range(NT):
                                pe.wait_ge(gi_mask.sem, gi_mask.after(layer, 4 * level + n + 1))
                                if level:
                                    pe.wait_ge(gi_up.sem, gi_up.after(layer, 4 * (level - 1) + n + 1))
                                for h in range(HEADS):
                                    last = pe.matmul(banks[Z_BANK[n]][:, h * P:(h + 1) * P], GAM[:, n, h, :],
                                                     GX[:, n, h, :] if level else mc(C_ID), start=True, stop=True)
                                last.then_inc(gi_z.step(), 1)
                            for n in range(NT if level else 0):
                                pe.wait_ge(gi_zc.sem, gi_zc.after(layer, 4 * (level - 1) + n + 1))
                                for h in range(HEADS):
                                    c0 = slice(h * P, (h + 1) * P)
                                    last = pe.matmul(cols(banks[2 + n][:, c0], level, 1), GY[:, n, h, :], cols(GT[:, n, h, :], level, 1),
                                                     start=True, stop=True)
                                    if level < LEVELS - 1:
                                        last = pe.matmul(cols(banks[2 + n][:, c0], level, 0), GT[:, n, h, :],
                                                         cols(GY[:, n, h, :], level, 0), start=True, stop=True)
                                last.then_inc(gi_xy.step(), 1)
                        for n in range(NT):
                            pe.wait_ge(gi_up.sem, gi_up.after(layer, 4 * LEVELS))
                            if n >= 2:
                                pe.wait_ge(gw_copied.sem, gw_copied.after(layer, n - 1))
                            for h in range(HEADS):
                                last = pe.matmul(banks[n % 2][:, h * P:(h + 1) * P], GKC[:, n, h, :], GX[:, n, h, :], start=True, stop=True)
                            last.then_inc(gw_mm.step(), 1)
                        pe.wait_ge(gw_copied.sem, gw_copied.after(layer, NT))
                        for n in range(NT):
                            a, b = slice(n * P, (n + 1) * P), n % 2
                            if n:
                                pe.wait_ge(gs_state.sem, gs_state.after(layer, 4 * n))
                            for h in range(HEADS):
                                c0 = slice(h * P, (h + 1) * P)
                                last = pe.matmul(banks[b][:, c0], GX[:, n, h, :], big[:, GV + h, a], start=True, stop=n == 0)
                                if n:
                                    last = pe.matmul(banks[b][:, c0], GY[:, n, h, :], GAM[:, 1 - b, h, :], start=False, stop=True)
                            last.then_inc(gs_v.step(), 1)
                            pe.wait_ge(gs_vn.sem, gs_vn.after(layer, n + 1))
                            if n < NT - 1:
                                for h in range(HEADS):
                                    last = pe.matmul(banks[2 + b][:, h * P:(h + 1) * P], big[:, GK + h, a], GT[:, b, h, :], start=True, stop=True)
                                last.then_inc(gs_ds.step(), 1)
                            for h in range(HEADS):
                                if n:
                                    pe.matmul(banks[4 + h][:, a], GAM[:, 1 - b, h, :], big[:, GQ + h, a], start=True, stop=False,
                                              skip_group_check=True)
                                last = pe.matmul(banks[4 + h][:, a], GT[:, b, h, :], GAQ[:, n, h, :], start=n == 0, stop=True,
                                                 skip_group_check=True)
                            last.then_inc(gs_o.step(), 1)

                        def part(m, ks, start):
                            if start:
                                split_ready(layer, R_MOUT + m)
                                pe.wait_ge(x_add.sem, x_add.freed(layer, 8 + m))
                            for k in ks:
                                if m == 0 and k in FIN_TILE:
                                    pe.wait_ge(fin_lo.sem, fin_lo.after(layer, FIN_TILE.index(k) + 1))
                                hi, lo = (w[m % 2][:, k * P:(k + 1) * P] for w in (w_hi, w_lo))
                                pe.matmul(banks[2 + m % 2], hi, h_hi[:, k, :], start=start and k == ks[0], stop=False, skip_group_check=True)
                                pe.matmul(banks[2 + m % 2], hi, h_lo[:, k, :], start=False, stop=False, skip_group_check=True)
                                last = pe.matmul(banks[2 + m % 2], lo, h_hi[:, k, :], start=False, stop=k == 5, skip_group_check=True)
                            if k == 5:
                                last.then_inc(unit_done.step(), 1)

                        finish(4, mc(C_ONES), banks[0])
                        finish(5, mc(C_ONES), banks[1])
                        part(0, (0, 1, 6, 7), True)
                        pe.wait_ge(fin_rs.sem, fin_rs.after(layer, 5))
                        finish(6, mc(C_ONES), banks[0])
                        pe.wait_ge(fin_rs.sem, fin_rs.after(layer, 6))
                        finish(7, mc(C_ONES), banks[1])
                        part(1, (0, 1, 6, 7), True)
                        part(0, (2, 3, 4, 5), False)
                        part(1, (2, 3, 4, 5), False)
                        for m in range(2, KT):
                            part(m, (0, 1, 6, 7, 2, 3, 4, 5), True)
                    norm_sum(layer, 2 * f)
                    per = 8 if ada else 4
                    step_in(layer, f, r_in, 0, ada, first=True)
                    with pe.Fori(0, 9) as i:
                        step_in(layer, f, r_in + per, 2, ada, i, 9)
                    step_in(layer, f, r_in + 10 * per, 20, False)
                    step_out(layer, f, r_out, 0, first=True)
                    with pe.Fori(0, 3) as i:
                        step_out(layer, f, r_out + 8, 2, i, 3)
            pe.wait_ge(sq_done.sem, sq_done.after(DEPTH - 1, 24))
            pe.matmul(banks[6], ones[:, :], sumsq[:, :], start=True, stop=True).then_inc(final_sum, 1)

        @block.scalar
        def _(act):
            act.preload_act_table_set("silu_and_others")
            act.wait_ge(small_loaded, 3 * 16)
            act.activation(c_act[:, 1, :], c_act[:, 0, :], ACT.Silu).then_inc(pro_act, 1)

            def high(layer, u, r, width, i=0, per=0, times=1):
                s = r % RAW
                wait_raw(act, layer, r, i, per)
                act.wait_ge(unit_done.sem, unit_done.freed(layer, u, i, 4))
                act.activation(w_hi[u % 2][:, 0:width], raw[s][:, 0:width], ACT.Copy).then_inc(hi_done.step(times), 1)

            def step_in(layer, f, u, r, chunk, ada, i=0, times=1, last=W8):
                order, per = (UNIT_AT, 8) if ada else (PLAIN, 4)
                for k in range(4):
                    if k < 3:
                        high(layer, u + k + 1, r + order[k + 1], W8, i, per, times)
                    else:
                        high(layer, u + 4, r + per, last, i, per, times)
                    if k % 2:
                        j = k // 2
                        act.wait_ge(unit_done.sem, unit_done.after(layer, u + 2 * j + 1, i, 4))
                        act.wait_ge(gated.sem, gated.freed(layer, 22 * f + chunk + j, i, 2))
                        act.activation(tmpA[:, j, :], banks[2 * j], ACT.Silu).then_inc(silu_done.step(times), 1)

            def step_out(layer, u, r, i=0, times=1, last=W11):
                for k in range(4):
                    if k < 3:
                        high(layer, u + k + 1, r + UNIT_AT[k + 1], W11, i, 8, times)
                    elif last:
                        high(layer, u + 4, r + 8, last, i, 8, times)

            def rsqrt(dst, src, scale, done):
                act.activation(dst, src, ACT.Ln, scale=scale, bias=EPS).then_inc(s_step.step(), 1)
                act.wait_ge(s_step.sem, s_step.now(layer))
                act.activation(dst, dst, ACT.Exp, scale=-0.5).then_inc(done.step(), 1)

            def norm(layer, n):
                act.preload_act_table_set("natural_log_exp_and_others")
                act.wait_ge(ms_sum.sem, ms_sum.after(layer, n + 1))
                rsqrt(tmpB[:, 0, :], banks[6], 1.0 / DM, rs_done)
                for k in range(KT):
                    act.wait_ge(norm_t.sem, norm_t.after(layer, 8 * n + k + 1))
                    shift = mods[:, 24 * n + k:24 * n + k + 1]
                    act.activation(h_hi[:, k, :], tmpA[:, k % 2, :], ACT.Identity, bias=shift).then_inc(norm_hi.step(), 1)

            def softplus_tail(a, src, stage_):
                act.activation(a, src, ACT.Abs).then_inc(s_step.step(), 1)
                act.wait_ge(s_step.sem, s_step.now(layer))
                act.activation(a, a, ACT.Exp, scale=-1.0).then_inc(s_step.step(), 1)
                act.wait_ge(s_step.sem, s_step.now(layer))
                act.activation(a, a, ACT.Ln, bias=1.0).then_inc(stage_.step(), 1)

            def square(k, bank):
                if k >= 4:
                    act.wait_ge(fin_y.sem, fin_y.after(layer, k - 1))
                act.activation(tmpB[:, k % 2, :], bank, ACT.Square).then_inc(fin_sq.step(), 1)

            def inverse(k, scale, bank):
                act.wait_ge(fin_sum.sem, fin_sum.after(layer, k + 1))
                rsqrt(tmpB[:, k % 2, :], bank, scale, fin_rs)

            def top(k, tile):
                act.wait_ge(fin_y.sem, fin_y.after(layer, k + 1))
                act.activation(h_hi[:, tile, :], tmpA[:, k % 2, :], ACT.Copy).then_inc(fin_hi.step(), 1)

            with act.Fori(0, DEPTH) as layer:
                for f, u_in, u_out, r_in, r_out, ada, _ in FFNS:
                    if f == 1:
                        norm(layer, 1)
                        for u in range(FEAT_UNITS + 8):
                            nxt = U_MIX + u + 1
                            width = W8 if u + 1 < FEAT_UNITS + 4 else 2 * TOK_B if u + 1 < FEAT_UNITS + 8 else W8
                            high(layer, nxt, R_MIX + u + 1, width)
                            if u < FEAT_UNITS:
                                act.wait_ge(unit_done.sem, unit_done.after(layer, U_MIX + u + 1))
                                if u < 12:
                                    act.wait_ge(conv_v.sem, conv_v.freed(layer, u))
                                    act.activation(padded[:, u % 2, 3:T + 3], banks[u % 2], ACT.Copy).then_inc(evac.step(), 1)
                                else:
                                    act.activation(big[:, u, :], banks[u % 2], ACT.Silu if u < SQ else ACT.Copy).then_inc(evac.step(), 1)
                                if 1 <= u <= 12:
                                    act.wait_ge(conv_v.sem, conv_v.after(layer, u))
                                    act.activation(big[:, u - 1, :], tmpB[:, (u - 1) % 2, :], ACT.Silu).then_inc(conv_silu.step(), 1)
                            if u == L2_AT + 10:
                                act.wait_ge(gd_row.sem, gd_row.after(layer, 8))
                                act.activation(squares[0:8, :], banks[6][0:8, :], ACT.Copy).then_inc(gd_rows.step(), 1)
                            if u == FEAT_UNITS + 3:
                                for n in range(NT):
                                    act.wait_ge(unit_done.sem, unit_done.after(layer, U_MIX + u + 1))
                                    act.activation(TFI[:, :, n, :], banks[2 + n][:, :].rearrange("p (a e) -> p a e", a=2), ACT.Copy).then_inc(s_step.step(), 1)
                                    act.wait_ge(s_step.sem, s_step.now(layer))
                        act.preload_act_table_set("natural_log_exp_and_others")
                        act.wait_ge(gd_rows.sem, gd_rows.after(layer, 1))
                        rsqrt(squares[0:8, :], squares[0:8, :], 1.0, gd_rs)
                        barrier(act, layer, 0)


                        def tail(h):
                            act.wait_ge(sb_zs.sem, sb_zs.after(layer, h + 1))
                            if h >= 2:
                                act.wait_ge(sb_o.sem, sb_o.after(layer, h - 1))
                            softplus_tail(SP[h % 2], Z[h % 2], sb_ln)

                        def weights(h):
                            act.wait_ge(sb_lw.sem, sb_lw.after(layer, h + 1))
                            act.activation(SP[h % 2], Z[h % 2], ACT.Exp).then_inc(sb_w.step(), 1)

                        act.wait_ge(gd_v.sem, gd_v.after(layer, 1))
                        softplus_tail(G_E, G_X, gd_s)
                        act.activation(G_EA, cur[:, Q_AL:Q_AL + 4], ACT.Exp).then_inc(s_step.step(), 1)
                        act.wait_ge(s_step.sem, s_step.now(layer))
                        tail(0)
                        act.wait_ge(gd_v.sem, gd_v.after(layer, 2))
                        act.activation(G_BETA.rearrange("p (n h) -> p n h", n=NT),
                                                G_LS.rearrange("p (n a h) -> p n a h", n=NT, a=2)[:, :, 0, :], ACT.Exp).then_inc(gd_s.step(), 1)
                        tail(1)
                        act.wait_ge(lb_v.sem, lb_v.after(layer, 1))
                        softplus_tail(lb_t, lb_d, lb_s)
                        softplus_tail(HE, TF, hg_s)
                        weights(0)
                        weights(1)
                        tail(2)
                        tail(3)
                        act.wait_ge(hg_v.sem, hg_v.after(layer, 1))
                        act.activation(HK, HK, ACT.Exp).then_inc(hg_ktok.step(), 1)
                        act.wait_ge(hg_v.sem, hg_v.after(layer, 2))
                        act.activation(HLF, HLF, ACT.Exp).then_inc(s_step.step(), 1)
                        act.wait_ge(s_step.sem, s_step.now(layer))
                        act.activation(HLF, HLF, ACT.Ln, bias=1.0).then_inc(hg_s.step(), 1)
                        weights(2)
                        weights(3)
                        inverse(0, 1.0 / 64, banks[6])
                        top(0, 0)

                        act.wait_ge(hg_sums.sem, hg_sums.after(layer, 1))
                        for b in range(2):
                            act.activation(HE[:, b * T:(b + 1) * T], banks[b], ACT.Copy).then_inc(hg_btok.step(), 1)
                        inverse(1, 1.0 / 64, banks[7])
                        act.wait_ge(hg_v.sem, hg_v.after(layer, 3))
                        act.activation(HLS, HLS, ACT.Exp).then_inc(hg_s.step(), 1)
                        for pr in range(2):
                            act.activation(HB[:, pr * T:(pr + 1) * T], banks[4 + pr], ACT.Copy).then_inc(s_step.step(), 1)
                            act.wait_ge(s_step.sem, s_step.now(layer))
                        act.activation(H_CD, HB.rearrange("p (a e) -> p a e", e=P)[:, :, P - 1], ACT.Exp).then_inc(s_step.step(), 1)
                        act.wait_ge(s_step.sem, s_step.now(layer))
                        act.activation(HQE, HB, ACT.Exp).then_inc(hg_bfeat.step(), 1)
                        top(1, 1)
                        for level in range(LEVELS):
                            act.wait_ge(hl_arg.sem, hl_arg.after(layer, level + 1))
                            act.wait_ge(hl_low.sem, hl_low.after(layer, level + 1))
                            act.activation(HEXP[level % 2], HEXP[level % 2], ACT.Exp).then_inc(hl_exp.step(), 1)
                        barrier(act, layer, 1)

                        act.wait_ge(ho_done.sem, ho_done.after(layer, 2))
                        for k in range(2):
                            square(2 + k, banks[6 + k])
                        act.wait_ge(gd_v.sem, gd_v.after(layer, 3))
                        act.activation(G_EG, G_G, ACT.Exp).then_inc(s_step.step(), 1)
                        act.wait_ge(s_step.sem, s_step.now(layer))
                        act.activation(G_EKD, G_TG, ACT.Exp).then_inc(s_step.step(), 1)
                        act.wait_ge(s_step.sem, s_step.now(layer))
                        act.activation(G_CD, G_TOT, ACT.Exp).then_inc(gd_s.step(), 1)
                        for k in range(2):
                            inverse(2 + k, 1.0 / 64, banks[4 + k])
                        for k in range(2):
                            top(2 + k, 6 + k)

                        def spread(n):
                            if n >= 2:
                                act.wait_ge(gc_row.sem, gc_row.after(layer, n - 1))
                            act.activation(GX[:, n % 2], nh(G_LA, n), ACT.Copy).then_inc(gc_bc.step(), 1)

                        def decays(n):
                            b = n % 2
                            act.wait_ge(gc_arg.sem, gc_arg.after(layer, n + 1))
                            act.activation(GY[:, b], GY[:, b], ACT.Exp, scale=-1.0).then_inc(s_step.step(), 1)
                            act.activation(GY[:, 2 + b], GY[:, 2 + b], ACT.Exp).then_inc(s_step.step(), 1)
                            if n >= 2:
                                act.wait_ge(gc_q.sem, gc_q.after(layer, n - 1))
                            act.wait_ge(s_step.sem, s_step.now(layer))
                            act.activation(flat(GT[:, b]), banks[b], ACT.Exp).then_inc(gc_exp.step(), 1)

                        act.wait_ge(gd_la.sem, gd_la.after(layer, 1))
                        spread(0)
                        spread(1)
                        for n in range(NT):
                            decays(n)
                            if n < NT - 2:
                                spread(n + 2)
                        for level in range(1, LEVELS):
                            for n in range(NT):
                                act.wait_ge(gi_z.sem, gi_z.after(layer, 4 * level + n + 1))
                                act.activation(flat(GT[:, n]), banks[Z_BANK[n]], ACT.Copy).then_inc(gi_zc.step(), 1)
                        for n in range(NT):
                            act.wait_ge(gw_mm.sem, gw_mm.after(layer, n + 1))
                            act.activation(flat(GY[:, n]), banks[n % 2], ACT.Copy).then_inc(gw_copied.step(), 1)
                        high(layer, U_MOUT + 1, R_MOUT + 1, W8)
                        act.wait_ge(gs_o.sem, gs_o.after(layer, NT))
                        square(4, banks[4])
                        square(5, banks[5])
                        inverse(4, 1.0 / 128, banks[0])
                        inverse(5, 1.0 / 128, banks[1])
                        square(6, banks[6])
                        top(4, 2)
                        square(7, banks[7])
                        top(5, 3)
                        inverse(6, 1.0 / 128, banks[0])
                        inverse(7, 1.0 / 128, banks[1])
                        top(6, 4)
                        top(7, 5)
                        act.preload_act_table_set("silu_and_others")
                        for m in range(1, KT):
                            high(layer, U_MOUT + m + 1, R_MOUT + m + 1, W8)
                    if f == 0:
                        high(layer, 0, R_IN1, W8)
                    norm(layer, 2 * f)
                    per = 8 if ada else 4
                    with act.Fori(0, 10) as i:
                        step_in(layer, f, u_in, r_in, 0, ada, i, 10)
                    step_in(layer, f, u_in + 40, r_in + 10 * per, 20, False, last=W11)
                    with act.Fori(0, 3) as i:
                        step_out(layer, u_out, r_out, i, 3)
                    step_out(layer, u_out + 12, r_out + 24, last=W8 if f == 0 else 0)
            act.preload_act_table_set("natural_log_exp_and_others")
            act.wait_ge(final_sum, 1)
            act.activation(tmpB[:, 0, :], banks[6], ACT.Ln, scale=1.0 / DM, bias=EPS).then_inc(final_rs, 1)
            act.wait_ge(final_rs, 1)
            act.activation(tmpB[:, 0, :], tmpB[:, 0, :], ACT.Exp, scale=-0.5).then_inc(final_rs, 1)

        @block.vector
        def _(dve):
            def low(layer, u, r, width, i=0, per=0, times=1):
                s = r % RAW
                dve.wait_ge(hi_done.sem, hi_done.after(layer, u + 1, i, 4))
                dve.tensor_tensor(w_lo[u % 2][:, 0:width], raw[s][:, 0:width],
                                               w_hi[u % 2][:, 0:width].bitcast(F32), ALU.subtract).then_inc(raw_used.step(times), 1)

            def ada_rows(piece, kk, link):
                for k2 in range(2):
                    k = 2 * kk + k2
                    w, s = piece[:, k2 * 512:(k2 + 1) * 512], c_act[:, 1, k:k + 1]
                    if k == 0:
                        ins = dve.tensor_scalar(ada_acc[:, :], w, s, None, ALU.mult)
                    else:
                        ins = dve.scalar_tensor_tensor(ada_acc[:, :], w, s, ada_acc[:, :], ALU.mult, ALU.add)
                    link(ins, k2)

            def ada_piece(layer, r, kk, g, i, times):
                wait_raw(dve, layer, r, i, 8)

                def link(ins, k2):
                    if k2 == 0:
                        ins.then_inc(ada_step.step(times), 1)
                        dve.wait_ge(ada_step.sem, ada_step.after(layer, 4 * g + kk + 1, i, 4))
                    else:
                        ins.then_inc(raw_used.step(times), 1)
                        if kk < 3:
                            dve.wait_ge(raw_used.sem, raw_used.after(layer, r + 1, i, 8))

                ada_rows(raw[r % RAW], kk, link)

            def ada_put(layer, g, dst, bias, i, times):
                dve.wait_ge(ada_sum.sem, ada_sum.after(layer, g + 1, i, 1))
                dve.tensor_tensor(dst, banks[7][:, 0:4], bias, ALU.add).then_inc(mod_step.step(times), 1)

            def step_in(layer, f, u, r, chunk, ada, i=0, times=1, last=W8):
                order, per = (UNIT_AT, 8) if ada else (PLAIN, 4)

                def gate(j):
                    dve.wait_ge(silu_done.sem, silu_done.after(layer, 22 * f + chunk + j + 1, i, 2))
                    dve.wait_ge(unit_done.sem, unit_done.after(layer, u + 2 * j + 2, i, 4))
                    dve.wait_ge(act_split.sem, act_split.freed(layer, 22 * f + chunk + j, i, 2))
                    dve.tensor_tensor(tmpB[:, j, :], banks[2 * j + 1], tmpA[:, j, :], ALU.mult).then_inc(gated.step(times), 1)

                if ada:
                    ada_piece(layer, r + ADA_AT[0], 0, 0, i, times)
                    ada_piece(layer, r + ADA_AT[1], 1, 0, i, times)
                low(layer, u + 1, r + order[1], W8, i, per, times)
                if ada:
                    ada_piece(layer, r + ADA_AT[2], 2, 0, i, times)
                    ada_piece(layer, r + ADA_AT[3], 3, 0, i, times)
                low(layer, u + 2, r + order[2], W8, i, per, times)
                gate(0)
                low(layer, u + 3, r + order[3], W8, i, per, times)
                if ada:
                    ada_put(layer, 0, mods[:, bass.ds(i * 4 + 16, 4)], cur[:, bass.ds(i * 4 + Q_ADAB, 4)], i, times)
                low(layer, u + 4, r + per, last, i, per, times)
                gate(1)

            def step_out(layer, f, u, r, m, g, put, i=0, times=1, last=W11):
                def add(j):
                    dve.wait_ge(unit_done.sem, unit_done.after(layer, u + 2 * j + 2, i, 4))
                    t = i * 2 + m + j
                    dve.scalar_tensor_tensor(X[:, bass.ds(t, 1), :] if times > 1 else X[:, m + j:m + j + 1, :],
                                                       banks[4 + j][:, :].unsqueeze(1),
                                                       gate_c[:, f, bass.ds(t, 1)] if times > 1 else gate_c[:, f, m + j:m + j + 1],
                                                       X[:, bass.ds(t, 1), :] if times > 1 else X[:, m + j:m + j + 1, :],
                                                       ALU.mult, ALU.add).then_inc(x_add.step(times), 1)

                ada_piece(layer, r + ADA_AT[0], 0, g, i, times)
                ada_piece(layer, r + ADA_AT[1], 1, g, i, times)
                low(layer, u + 1, r + UNIT_AT[1], W11, i, 8, times)
                ada_piece(layer, r + ADA_AT[2], 2, g, i, times)
                ada_piece(layer, r + ADA_AT[3], 3, g, i, times)
                low(layer, u + 2, r + UNIT_AT[2], W11, i, 8, times)
                add(0)
                low(layer, u + 3, r + UNIT_AT[3], W11, i, 8, times)
                dst, bias = put(i, times > 1)
                ada_put(layer, g, dst, bias, i, times)
                if last:
                    low(layer, u + 4, r + 8, last, i, 8, times)
                add(1)

            def norm(layer, n):
                dve.wait_ge(mod_step.sem, mod_step.after(layer, {0: 0, 1: 14, 2: 14}[n]))
                a = mods[:, 24 * n + 8:24 * n + 16]
                dve.scalar_tensor_tensor(mod_a[:, :], a, 1.0, cur[:, Q_GAIN + 8 * n:Q_GAIN + 8 * n + 8], ALU.add, ALU.mult).then_inc(v_step.step(), 1)
                dve.wait_ge(v_step.sem, v_step.now(layer))
                dve.wait_ge(rs_done.sem, rs_done.after(layer, n + 1))
                for k in range(KT + 1):
                    if k < KT:
                        if k >= 2:
                            dve.wait_ge(norm_lo.sem, norm_lo.freed(layer, 8 * n + k))
                        dve.scalar_tensor_tensor(tmpA[:, k % 2, :], X[:, k, :], mod_a[:, k:k + 1], tmpB[:, 0, :],
                                                            ALU.mult, ALU.mult).then_inc(norm_t.step(), 1)
                    if k:
                        j = k - 1
                        dve.wait_ge(norm_hi.sem, norm_hi.after(layer, 8 * n + j + 1))
                        dve.scalar_tensor_tensor(h_lo[:, j, :], tmpA[:, j % 2, :], mods[:, 24 * n + j:24 * n + j + 1],
                                                             h_hi[:, j, :].bitcast(F32), ALU.add, ALU.subtract).then_inc(norm_lo.step(), 1)

            def squares_of(k, src):
                if k >= 2:
                    dve.wait_ge(fin_lo.sem, fin_lo.after(layer, k - 1))
                dve.tensor_copy(tmpA[:, k % 2, :], src).then_inc(v_step.step(), 1)
                dve.wait_ge(v_step.sem, v_step.now(layer))
                dve.tensor_tensor(tmpB[:, k % 2, :], tmpA[:, k % 2, :], tmpA[:, k % 2, :], ALU.mult).then_inc(fin_sq.step(), 1)

            def scaled(k, gain, gate=None, src=None):
                y = tmpA[:, k % 2, :]
                if src is not None and k >= 4:
                    dve.wait_ge(fin_lo.sem, fin_lo.after(layer, k - 1))
                dve.wait_ge(fin_rs.sem, fin_rs.after(layer, k + 1))
                ins = dve.scalar_tensor_tensor(y, y if src is None else src, cur[:, gain:gain + 1], tmpB[:, k % 2, :], ALU.mult, ALU.mult)
                if gate is not None:
                    ins.then_inc(v_step.step(), 1)
                    dve.wait_ge(v_step.sem, v_step.now(layer))
                    ins = dve.tensor_tensor(y, y, gate, ALU.mult)
                ins.then_inc(fin_y.step(), 1)

            def rest(k, tile):
                dve.wait_ge(fin_hi.sem, fin_hi.after(layer, k + 1))
                dve.tensor_tensor(h_lo[:, tile, :], tmpA[:, k % 2, :], h_hi[:, tile, :].bitcast(F32), ALU.subtract).then_inc(fin_lo.step(), 1)

            dve.memset(ones[:, :], 1.0).then_inc(pro_ones, 1)
            dve.wait_ge(pro_act, 1)
            n_v = [0]

            def pro_link(ins, k2):
                n_v[0] += 1
                ins.then_inc(pro_v, 1)
                if n_v[0] % 8:
                    dve.wait_ge(pro_v, n_v[0])

            for g in range(4):
                for kk in range(4):
                    if kk % 2 == 0:
                        dve.wait_ge(pro_loaded[2 * g + kk // 2], 16)
                    ada_rows(PRO[g][:, kk, :], kk, pro_link)
                dve.wait_ge(pro_sum, g + 1)
                dve.tensor_tensor(mods_next[:, 4 * g:4 * g + 4], banks[7][:, 0:4],
                                  PRM[:, DEPTH - 1, Q_ADAB + 56 + 4 * g:Q_ADAB + 60 + 4 * g], ALU.add).then_inc(pro_mod, 1)
            dve.wait_ge(pro_mod, 4)

            with dve.Fori(0, DEPTH) as layer:
                for f, u_in, u_out, r_in, r_out, ada, g in FFNS:
                    if f == 0:
                        low(layer, 0, R_IN1, W8)
                        dve.wait_ge(mod_step.sem, mod_step.after(layer, 0))
                        dve.tensor_copy(cur[:, :].unsqueeze(1), PRM[:, bass.ds(layer, 1), :]).then_inc(v_step.step(), 1)
                        dve.wait_ge(v_step.sem, v_step.now(layer))
                        dve.tensor_copy(mods[:, 0:16], mods_next[:, :]).then_inc(v_step.step(), 1)
                        dve.wait_ge(v_step.sem, v_step.now(layer))
                    if f == 1:
                        norm(layer, 1)
                        for u in range(FEAT_UNITS + 8):
                            width = W8 if u + 1 < FEAT_UNITS + 4 else 2 * TOK_B if u + 1 < FEAT_UNITS + 8 else W8
                            low(layer, U_MIX + u + 1, R_MIX + u + 1, width)
                            if u < 12:
                                dve.wait_ge(evac.sem, evac.after(layer, u + 1))
                                dve.wait_ge(conv_silu.sem, conv_silu.freed(layer, u))
                                acc, w = tmpB[:, u % 2, :], lambda tap: cur[:, Q_CONV + 4 * u + tap:Q_CONV + 4 * u + tap + 1]
                                dve.tensor_scalar(acc, padded[:, u % 2, 0:T], w(0), None, ALU.mult).then_inc(v_step.step(), 1)
                                dve.wait_ge(v_step.sem, v_step.now(layer))
                                for tap in (1, 2, 3):
                                    ins = dve.scalar_tensor_tensor(acc, padded[:, u % 2, tap:T + tap], w(tap), acc, ALU.mult, ALU.add)
                                    if tap < 3:
                                        ins.then_inc(v_step.step(), 1)
                                        dve.wait_ge(v_step.sem, v_step.now(layer))
                                    else:
                                        ins.then_inc(conv_v.step(), 1)
                        for n in range(NT):
                            dve.wait_ge(unit_done.sem, unit_done.after(layer, U_MIX + FEAT_UNITS + 8))
                            b = banks[(6 + n) % 8]
                            dve.tensor_copy(TV[:, n * 256:(n + 1) * 256], b[:, 0:256])
                            dve.tensor_copy(BA[:, 8 * n:8 * n + 8], b[:, 256:264]).then_inc(tok_copied.step(), 1)
                        barrier(dve, layer, 0)

                        dve.wait_ge(mixer_constants, layer * 32 + 32)

                        def scaled_scores(h):
                            dve.wait_ge(sb_z.sem, sb_z.after(layer, h + 1))
                            if h >= 2:
                                dve.wait_ge(sb_w.sem, sb_w.after(layer, h - 1))
                            for b, c0, w in ((0, 0, 512), (1, 512, 384), (2, 896, 384)):
                                ins = dve.tensor_scalar(Z[h % 2][:, c0:c0 + w], banks[3 * (h % 2) + b][:, 0:w], 64 ** -0.5, None, ALU.mult)
                                ins.then_inc(v_step.step() if b < 2 else sb_zs.step(), 1)

                        def softplus(h):
                            sp = SP[h % 2]
                            dve.wait_ge(sb_ln.sem, sb_ln.after(layer, h + 1))
                            dve.scalar_tensor_tensor(sp, Z[h % 2], 0.0, sp, ALU.max, ALU.add).then_inc(v_step.step(), 1)
                            dve.wait_ge(v_step.sem, v_step.now(layer))
                            for kb in range(NT):
                                a = sp[:, SB_OFF[kb]:SB_OFF[kb] + P]
                                ins = dve.tensor_tensor(a, a, MC[:, C_STRICT, :], ALU.mult)
                                ins.then_inc(v_step.step() if kb < NT - 1 else sb_sp.step(), 1)

                        def log_weights(h):
                            dve.wait_ge(sb_cum.sem, sb_cum.after(layer, h + 1))
                            for b, c0, w in ((0, 0, 512), (1, 512, 384), (2, 896, 384)):
                                a = Z[h % 2][:, c0:c0 + w]
                                dve.tensor_tensor(a, banks[3 * (h % 2) + b][:, 0:w], a, ALU.add).then_inc(v_step.step(), 1)
                            dve.wait_ge(v_step.sem, v_step.now(layer))
                            for kb in range(NT):
                                a = Z[h % 2][:, SB_OFF[kb]:SB_OFF[kb] + P]
                                ins = dve.tensor_tensor(a, a, MC[:, C_SNEG, :], ALU.add)
                                ins.then_inc(v_step.step() if kb < NT - 1 else sb_lw.step(), 1)

                        ba, gx = (a.rearrange("p (n e) -> p n e", n=NT) for a in (BA, G_X))
                        dve.tensor_copy(gx[:, :, 0:4], ba[:, :, 0:4]).then_inc(v_step.step(), 1)
                        dve.tensor_tensor(gx[:, :, 4:8], ba[:, :, 4:8], cur[:, Q_DT:Q_DT + 4].unsqueeze(1).to_broadcast([P, NT, 4]), ALU.add).then_inc(v_step.step(), 1)
                        dve.wait_ge(v_step.sem, v_step.now(layer))
                        dve.tensor_scalar(gx[:, :, 4:8], gx[:, :, 4:8], -1.0, None, ALU.mult).then_inc(gd_v.step(), 1)
                        scaled_scores(0)
                        dve.wait_ge(gd_s.sem, gd_s.after(layer, 1))
                        dve.wait_ge(gd_v.sem, gd_v.after(layer, 1))
                        dve.scalar_tensor_tensor(G_LS, G_X, 0.0, G_E, ALU.min, ALU.subtract).then_inc(gd_v.step(), 1)
                        dve.wait_ge(gd_v.sem, gd_v.after(layer, 2))
                        dve.wait_ge(gd_s.sem, gd_s.after(layer, 2))
                        gn = lambda a: a.rearrange("p (n h) -> p n h", n=NT)
                        dve.tensor_tensor(gn(G_LA), G_LS.rearrange("p (n e) -> p n e", n=NT)[:, :, 4:8],
                                                    G_EA.unsqueeze(1).to_broadcast([P, NT, 4]), ALU.mult).then_inc(gd_la.step(), 1)
                        scaled_scores(1)
                        dve.tensor_tensor(lb_d, lb_in[:, 256:512], lb_in[:, 0:256], ALU.subtract).then_inc(v_step.step(), 1)
                        dve.wait_ge(v_step.sem, v_step.now(layer))
                        dve.tensor_scalar(LB[:, 1, :], lb_d, -1.0, None, ALU.mult).then_inc(lb_v.step(), 1)
                        softplus(0)
                        softplus(1)
                        dve.wait_ge(lb_v.sem, lb_v.after(layer, 1))
                        dve.wait_ge(lb_s.sem, lb_s.after(layer, 1))
                        for a, s in ((0, lb_d), (1, LB[:, 1, :])):
                            dve.scalar_tensor_tensor(LB[:, a, :], s, 0.0, lb_t, ALU.min, ALU.subtract).then_inc(v_step.step(), 1)
                        dve.wait_ge(v_step.sem, v_step.now(layer))
                        fl = cur[:, Q_FL:Q_FL + 1]
                        dve.tensor_scalar(LB[:, 0, :], LB[:, 0, :], fl, cur[:, Q_NEG:Q_NEG + 1], ALU.mult, ALU.add).then_inc(v_step.step(), 1)
                        dve.tensor_scalar(LB[:, 1, :], LB[:, 1, :], fl, None, ALU.mult).then_inc(v_step.step(), 1)
                        n4 = lambda a: a.rearrange("p (n e) -> p n e", n=NT)
                        loglb, log1mlb = (LB[:, a:a + 1, :].to_broadcast([P, NT, 256]) for a in (0, 1))
                        log_weights(0)
                        dve.wait_ge(hg_s.sem, hg_s.after(layer, 1))
                        dve.scalar_tensor_tensor(HLS, TF, 0.0, HE, ALU.min, ALU.subtract).then_inc(v_step.step(), 1)
                        dve.wait_ge(v_step.sem, v_step.now(layer))
                        dve.tensor_tensor(HK, HLS, TF, ALU.subtract).then_inc(v_step.step(), 1)
                        dve.wait_ge(v_step.sem, v_step.now(layer))
                        log_weights(1)
                        scaled_scores(2)
                        dve.tensor_tensor(n4(HK), n4(HK), log1mlb, ALU.add).then_inc(hg_v.step(), 1)
                        scaled_scores(3)
                        softplus(2)
                        dve.tensor_tensor(n4(HLS), n4(HLS), log1mlb, ALU.add).then_inc(v_step.step(), 1)
                        dve.wait_ge(v_step.sem, v_step.now(layer))
                        dve.tensor_tensor(n4(HE), n4(HLS), loglb, ALU.max).then_inc(v_step.step(), 1)
                        dve.tensor_tensor(n4(HLF), n4(HLS), loglb, ALU.min).then_inc(v_step.step(), 1)
                        dve.wait_ge(v_step.sem, v_step.now(layer))
                        dve.tensor_tensor(HLF, HLF, HE, ALU.subtract).then_inc(hg_v.step(), 1)
                        softplus(3)
                        dve.wait_ge(sb_o.sem, sb_o.after(layer, 2))
                        squares_of(0, banks[6])
                        log_weights(2)
                        dve.wait_ge(hg_s.sem, hg_s.after(layer, 2))
                        dve.tensor_tensor(HLF, HLF, HE, ALU.add).then_inc(hg_logf.step(), 1)
                        log_weights(3)
                        scaled(0, Q_SB)
                        rest(0, 0)
                        dve.wait_ge(sb_o.sem, sb_o.after(layer, HEADS))
                        squares_of(1, banks[7])

                        dve.wait_ge(hg_btok.sem, hg_btok.after(layer, 2))
                        for b in range(2):
                            a = slice(b * T, (b + 1) * T)
                            ins = dve.tensor_tensor(HLS[:, a], banks[2 + b], HE[:, a], ALU.subtract)
                            if b == 0:
                                ins.then_inc(v_step.step(), 1)
                        ins.then_inc(hg_v.step(), 1)
                        scaled(1, Q_SB)
                        rest(1, 1)
                        dve.wait_ge(hg_s.sem, hg_s.after(layer, 3))
                        dve.wait_ge(hg_ktok.sem, hg_ktok.after(layer, 1))
                        dve.tensor_tensor(HKD, HLS, HK, ALU.mult).then_inc(hg_kdec.step(), 1)
                        dve.wait_ge(hg_turned.sem, hg_turned.after(layer, 1))
                        for pr in range(2):
                            ins = dve.tensor_copy(HKT[:, pr * T:(pr + 1) * T], banks[6 + pr])
                            if pr == 0:
                                ins.then_inc(v_step.step(), 1)
                        ins.then_inc(hg_kT.step(), 1)
                        def put(level):
                            upper = lambda a: a.rearrange("p (n m s w) -> p n m s w", n=NT, s=2, w=1 << level)[:, :, :, 1, :]
                            mask = cols(MC[:, C_MT + level, :], level, 1).bitcast(I32).unsqueeze(1).to_broadcast([P, NT, P >> level + 1, 1 << level])
                            for h in range(HEADS):
                                src = banks[2 * (level % 2) + h // 2].rearrange("p (n h m w) -> p n h m w", n=NT, h=2, w=1 << level)
                                ins = dve.copy_predicated(upper(HAT[:, h, :]), mask, src[:, :, h % 2, :, :])
                                ins.then_inc(v_step.step() if h < 3 else hl_put.step(), 1)

                        def decays(level):
                            ref = cols(HB, level, 0)[:, :, (1 << level) - 1:1 << level].to_broadcast([P, 1024 >> level + 1, 1 << level])
                            upper = cols(HEXP[level % 2], level, 1)
                            dve.tensor_tensor(upper, cols(HB, level, 1), ref, ALU.subtract).then_inc(hl_arg.step(), 1)

                        def queries(level):
                            dve.wait_ge(hl_exp.sem, hl_exp.after(layer, level + 1))
                            for hh in range(2):
                                p0 = 64 * hh
                                upper = lambda a: a[p0:p0 + 64, :].rearrange("p (c m s w) -> p c m s w", c=8, s=2, w=1 << level)[:, :, :, 1, :]
                                dst = HQ2[level % 2][p0:p0 + 64, :, hh, :].rearrange("p c (m w) -> p c m w", w=1 << level)
                                dve.tensor_tensor(dst, upper(HEXP[level % 2]), upper(HQT), ALU.mult).then_inc(v_step.step() if hh == 0 else hl_h.step(), 1)

                        dve.wait_ge(hg_kT.sem, hg_kT.after(layer, 1))
                        dve.tensor_tensor(HPROD, HQT, HKT, ALU.mult).then_inc(hl_prod.step(), 1)
                        dve.wait_ge(hg_bfeat.sem, hg_bfeat.after(layer, 1))
                        decays(0)
                        decays(1)
                        dve.wait_ge(hl_diag.sem, hl_diag.after(layer, 1))
                        for h in range(HEADS):
                            ident = MC[:, C_ID:C_ID + 1, :].to_broadcast([P, NT, P])
                            own = banks[7][:, 8 * (h // 2):8 * (h // 2) + 8].rearrange("p (n h) -> p n h", h=2)[:, :, h % 2].unsqueeze(2)
                            dve.tensor_tensor(HAT[:, h, :].rearrange("p (n e) -> p n e", n=NT), ident, own.to_broadcast([P, NT, P]),
                                              ALU.mult).then_inc(v_step.step(), 1)
                        dve.wait_ge(v_step.sem, v_step.now(layer))
                        dve.wait_ge(hg_zero.sem, hg_zero.after(layer, 1))
                        queries(0)
                        dve.wait_ge(hg_ds.sem, hg_ds.after(layer, 1))
                        bd = MC[:, C_BD:C_BD + 1, :].to_broadcast([P, NT, P])
                        for pr in range(2):
                            ins = dve.tensor_tensor(HLS[:, pr * T:(pr + 1) * T].rearrange("p (n e) -> p n e", n=NT),
                                                    banks[4 + pr][:, :].rearrange("p (n e) -> p n e", n=NT), bd, ALU.mult)
                            if pr == 0:
                                ins.then_inc(v_step.step(), 1)
                                dve.wait_ge(v_step.sem, v_step.now(layer))
                        ins.then_inc(hg_ds_read.step(), 1)
                        dve.wait_ge(hg_ds_read.sem, hg_ds_read.after(layer, 1))
                        ds = HLS.rearrange("p (a n e) -> p a n e", a=2, n=NT)
                        for n in range(1, NT):
                            for pr in range(2):
                                if n == 1:
                                    ins = dve.tensor_copy(HS[:, pr, 1, :], ds[:, pr, 0, :])
                                else:
                                    ins = dve.scalar_tensor_tensor(HS[:, pr, n, :], HS[:, pr, n - 1, :], H_CD[:, 4 * pr + n - 1:4 * pr + n],
                                                                   ds[:, pr, n - 1, :], ALU.mult, ALU.add)
                                if n < NT - 1 or pr == 0:
                                    ins.then_inc(v_step.step(), 1)
                                    dve.wait_ge(v_step.sem, v_step.now(layer))
                        ins.then_inc(hg_state.step(), 1)
                        dve.wait_ge(hl_h.sem, hl_h.after(layer, 1))
                        dve.wait_ge(hl_k.sem, hl_k.after(layer, 1))
                        decays(2)
                        q_ = lambda a, b: dve.tensor_tensor(HQE[:, a:b], HQE[:, a:b], HQT[:, a:b], ALU.mult)
                        for level in range(1, LEVELS):
                            if level >= 2:
                                dve.wait_ge(hl_gram.sem, hl_gram.after(layer, level - 1))
                            queries(level)
                            dve.wait_ge(hl_h.sem, hl_h.after(layer, level + 1))
                            dve.wait_ge(hl_k.sem, hl_k.after(layer, level + 1))
                            dve.wait_ge(hl_gram.sem, hl_gram.after(layer, level))
                            if level > 1:
                                dve.wait_ge(hl_put.sem, hl_put.after(layer, level - 1))
                            if level < LEVELS - 2:
                                decays(level + 2)
                            elif level == LEVELS - 2:
                                q_(0, T).then_inc(v_step.step(), 1)
                            else:
                                q_(T, T + 256).then_inc(v_step.step(), 1)
                            put(level - 1)
                        dve.wait_ge(hl_put.sem, hl_put.after(layer, LEVELS - 1))
                        dve.wait_ge(hl_gram.sem, hl_gram.after(layer, LEVELS))
                        q_(T + 256, 2 * T).then_inc(hg_qe.step(), 1)
                        put(LEVELS - 1)
                        barrier(dve, layer, 1)

                        dve.wait_ge(gd_cum.sem, gd_cum.after(layer, 1))
                        dve.tensor_copy(G_G, banks[0][:, 0:16]).then_inc(v_step.step(), 1)
                        dve.tensor_copy(G_TOT, banks[1][:, 0:16]).then_inc(v_step.step(), 1)
                        dve.wait_ge(v_step.sem, v_step.now(layer))
                        dve.tensor_tensor(G_TG, G_TOT, G_G, ALU.subtract).then_inc(gd_v.step(), 1)
                        dve.wait_ge(gd_s.sem, gd_s.after(layer, 3))
                        dve.scalar_tensor_tensor(G_CB, G_EG, -1.0, G_BETA, ALU.mult, ALU.mult).then_inc(gd_cols.step(), 1)
                        for k in range(2):
                            scaled(2 + k, Q_HG, big[:, HG + k, :], banks[6 + k])

                        def exponents(n):
                            b = n % 2
                            row = lambda t: MC[:, t:t + 1, :].to_broadcast([P, HEADS, P])
                            arg = GX[:, 2 + b]
                            dve.wait_ge(gc_row.sem, gc_row.after(layer, n + 1))
                            if n >= 2:
                                dve.wait_ge(gc_kv.sem, gc_kv.after(layer, n - 1))
                            dve.tensor_tensor(arg, banks[b][:, :].rearrange("p (h e) -> p h e", h=HEADS), nh(G_G, n), ALU.subtract).then_inc(v_step.step(), 1)
                            dve.wait_ge(v_step.sem, v_step.now(layer))
                            dve.tensor_tensor(GY[:, b], arg, row(C_POSA), ALU.add).then_inc(v_step.step(), 1)
                            dve.tensor_tensor(GY[:, 2 + b], arg, row(C_NEGD), ALU.add).then_inc(gc_arg.step(), 1)

                        for k in range(2):
                            rest(2 + k, 6 + k)
                        for t in range(8):
                            dve.wait_ge(gd_l2x.sem, gd_l2x.after(layer, t + 1))
                            dve.scalar_tensor_tensor(big[:, t, :], big[:, t, :], 1.0 if t < 4 else float(128 ** -0.5), banks[2 + t % 2],
                                                               ALU.mult, ALU.mult).then_inc(gd_l2.step(), 1)
                        dve.wait_ge(gd_l2.sem, gd_l2.after(layer, 8))
                        dve.wait_ge(gd_cols.sem, gd_cols.after(layer, 1))
                        for n in range(NT):
                            a, b = slice(n * P, (n + 1) * P), n % 2
                            pk = lambda bk: banks[bk][:, :].rearrange("p (h e) -> p h e", h=HEADS)
                            if n == 0:
                                exponents(0)
                                exponents(1)
                            dve.wait_ge(gc_pairs.sem, gc_pairs.after(layer, n + 1))
                            dve.tensor_tensor(GKC[:, n], pk(6), nh(G_CB, n), ALU.mult).then_inc(v_step.step(), 1)
                            dve.tensor_tensor(big[:, GK:GK + 4, a], pk(6), nh(G_EKD, n), ALU.mult).then_inc(v_step.step(), 1)
                            dve.tensor_tensor(big[:, GV:GV + 4, a], pk(7), nh(G_BETA, n), ALU.mult).then_inc(gc_turned.step(), 1)
                            dve.wait_ge(gc_exp.sem, gc_exp.after(layer, n + 1))
                            dve.tensor_tensor(GA[:, n], pk(2 + b), GY[:, b], ALU.mult).then_inc(gc_a.step(), 1)
                            dve.tensor_tensor(GAQ[:, n], pk(4 + b), GY[:, 2 + b], ALU.mult).then_inc(gc_kv.step(), 1)
                            dve.tensor_tensor(big[:, GQ:GQ + 4, a], big[:, GQ:GQ + 4, a], GT[:, b], ALU.mult).then_inc(gc_q.step(), 1)
                            if n < NT - 2:
                                exponents(n + 2)
                        for level in range(LEVELS):
                            for n in range(NT):
                                if level == 0:
                                    idn = MC[:, C_ID:C_ID + 1, :].to_broadcast([P, HEADS, P])
                                    dve.wait_ge(gi_z.sem, gi_z.after(layer, n + 1))
                                    dve.tensor_tensor(GX[:, n], idn, banks[Z_BANK[n]][:, :].rearrange("p (h e) -> p h e", h=HEADS), ALU.subtract).then_inc(v_step.step(), 1)
                                    dve.tensor_tensor(GY[:, n], idn, GAM[:, n], ALU.subtract).then_inc(gi_up.step(), 1)
                                    continue
                                dve.wait_ge(gi_xy.sem, gi_xy.after(layer, 4 * (level - 1) + n + 1))
                                if level < LEVELS - 1:
                                    y = cols(flat(GY[:, n]), level, 0)
                                    dve.tensor_tensor(y, y, cols(banks[2 + n], level, 0), ALU.subtract).then_inc(v_step.step(), 1)
                                x_ = cols(flat(GX[:, n]), level, 1)
                                dve.tensor_tensor(x_, x_, cols(banks[2 + n], level, 1), ALU.subtract).then_inc(gi_up.step(), 1)
                        for n in range(NT):
                            b = n % 2
                            dve.wait_ge(gs_v.sem, gs_v.after(layer, n + 1))
                            if n >= 2:
                                dve.wait_ge(gs_o.sem, gs_o.after(layer, n - 1))
                            dve.tensor_copy(flat(GT[:, b]), banks[b]).then_inc(gs_vn.step(), 1)
                            if n < NT - 1:
                                dve.wait_ge(gs_ds.sem, gs_ds.after(layer, n + 1))
                                for h in range(HEADS):
                                    dst, inc = GAM[:, b, h, :], banks[2 + b][:, h * P:(h + 1) * P]
                                    if n == 0:
                                        ins = dve.tensor_copy(dst, inc)
                                    else:
                                        dve.wait_ge(gs_state.sem, gs_state.after(layer, 4 * n))
                                        ins = dve.scalar_tensor_tensor(dst, GAM[:, 1 - b, h, :], G_CD[:, 4 * n + h:4 * n + h + 1], inc,
                                                                       ALU.mult, ALU.add)
                                    ins.then_inc(gs_state.step(), 1)
                        low(layer, U_MOUT + 1, R_MOUT + 1, W8)
                        for k in range(4, 8):
                            if k >= 6:
                                rest(k - 2, k - 4)
                            scaled(k, Q_GD, big[:, GZ + k - 4, :], banks[k])
                        rest(6, 4)
                        rest(7, 5)
                        for m in range(KT):
                            if m:
                                low(layer, U_MOUT + m + 1, R_MOUT + m + 1, W8)
                            dve.wait_ge(unit_done.sem, unit_done.after(layer, U_MOUT + m + 1))
                            dve.scalar_tensor_tensor(X[:, m, :], banks[2 + m % 2], mods[:, 40 + m:41 + m], X[:, m, :],
                                                     ALU.mult, ALU.add).then_inc(x_add.step(), 1)
                    norm(layer, 2 * f)
                    per = 8 if ada else 4
                    with dve.Fori(0, 10) as i:
                        step_in(layer, f, u_in, r_in, 0, ada, i, 10)
                    dve.wait_ge(mod_step.sem, mod_step.after(layer, 10 if f == 0 else 14))
                    dve.tensor_scalar(gate_c[:, f, :], mods[:, 16 + 48 * f:24 + 48 * f], 0.5, None, ALU.mult).then_inc(v_step.step(), 1)
                    dve.wait_ge(v_step.sem, v_step.now(layer))
                    step_in(layer, f, u_in + 40, r_in + 10 * per, 20, False, last=W11)

                    def put(i, loop, f=f):
                        if f == 0:
                            return ((mods[:, bass.ds(i * 4 + 56, 4)], cur[:, bass.ds(i * 4 + Q_ADAB + 40, 4)]) if loop
                                    else (mods[:, 68:72], cur[:, Q_ADAB + 52:Q_ADAB + 56]))
                        return ((mods_next[:, bass.ds(i * 4, 4)], cur[:, bass.ds(i * 4 + Q_ADAB + 56, 4)]) if loop
                                else (mods_next[:, 12:16], cur[:, Q_ADAB + 68:Q_ADAB + 72]))

                    with dve.Fori(0, 3) as i:
                        step_out(layer, f, u_out, r_out, 0, g, put, i, 3)
                    step_out(layer, f, u_out + 12, r_out + 24, 6, g + 3, put, last=W8 if f == 0 else 0)
            dve.wait_ge(final_rs, 2)
            for k in range(KT):
                dve.scalar_tensor_tensor(X[:, k, :], X[:, k, :], fin_gain[:, k:k + 1], tmpB[:, 0, :],
                                         ALU.mult, ALU.mult).then_inc(final_done, 1)

        @block.gpsimd
        def _(pool):
            for s in used:
                if s.free and s is not sq_done:
                    pool.sem_inc(s.sem, s.free)
            pool.memset(padded[:, :, 0:3], 0.0)
            pool.wait_ge(x_loaded, 2 * 16)

            def square(layer, s, m, i=0, times=1):
                pool.wait_ge(x_add.sem, x_add.after(layer, 8 * s + m + 1, i, 1))
                src = X[:, bass.ds(i + m, 1), :] if times > 1 else X[:, m:m + 1, :]
                if m == 0:
                    pool.tensor_tensor(sumsq[:, :].unsqueeze(1), src, src, ALU.mult).then_inc(sq_done.step(), 1)
                    return
                pool.wait_ge(sq_done.sem, sq_done.after(layer, 8 * s + m, i, 1))
                pool.tensor_tensor(squares[:, :].unsqueeze(1), src, src, ALU.mult).then_inc(sq_step.step(times), 1)
                pool.wait_ge(sq_step.sem, sq_step.after(layer, 7 * s + m, i, 1))
                pool.tensor_tensor(sumsq[:, :], sumsq[:, :], squares[:, :], ALU.add).then_inc(sq_done.step(times), 1)

            pool.tensor_tensor(sumsq[:, :], X[:, 0, :], X[:, 0, :], ALU.mult).then_inc(sq_done.sem, 1)
            for m in range(1, KT):
                pool.wait_ge(sq_done.sem, m)
                pool.tensor_tensor(squares[:, :], X[:, m, :], X[:, m, :], ALU.mult).then_inc(pro_sq, 1)
                pool.wait_ge(pro_sq, m)
                pool.tensor_tensor(sumsq[:, :], sumsq[:, :], squares[:, :], ALU.add).then_inc(sq_done.sem, 1)

            with pool.Fori(0, DEPTH) as layer:
                for f, *_ in FFNS:
                    if f == 1:
                        for t in range(8):
                            pool.wait_ge(conv_silu.sem, conv_silu.after(layer, t + 1))
                            if t >= 2:
                                pool.wait_ge(gd_row.sem, gd_row.after(layer, t - 1))
                            pool.tensor_tensor(tmpA[:, t % 2, :], big[:, t, :], big[:, t, :], ALU.mult).then_inc(gd_sq.step(), 1)
                        zeros = MC[:, C_PICK:C_PICK + 1, P // 2:P].to_broadcast([P, 16, 64])
                        for k, dst in enumerate((spare, HX[:, 6144:7168], HX[:, 7168:8192])):
                            if k == 1:
                                pool.wait_ge(sb_o.sem, sb_o.after(layer, HEADS))
                            z = pool.tensor_tensor(dst.rearrange("p (c e) -> p c e", e=64), zeros, zeros, ALU.mult)
                            z.then_inc(p_step.step() if k < 2 else hg_zero.step(), 1)
                        def lower(level):
                            if level >= 2:
                                pool.wait_ge(hl_h.sem, hl_h.after(layer, level - 1))
                                pool.wait_ge(hl_k.sem, hl_k.after(layer, level - 1))
                            ref = cols(HB, level, 0)[:, :, (1 << level) - 1:1 << level].to_broadcast([P, 1024 >> level + 1, 1 << level])
                            pool.tensor_tensor(cols(HEXP[level % 2], level, 0), ref, cols(HB, level, 0), ALU.subtract).then_inc(hl_low.step(), 1)

                        pool.wait_ge(hg_zero.sem, hg_zero.after(layer, 1))
                        pool.wait_ge(hg_bfeat.sem, hg_bfeat.after(layer, 1))
                        pool.wait_ge(hg_kdec.sem, hg_kdec.after(layer, 1))
                        lower(0)
                        pool.wait_ge(hg_kT.sem, hg_kT.after(layer, 1))
                        for level in range(LEVELS):
                            if level >= 2:
                                pool.wait_ge(hl_gram.sem, hl_gram.after(layer, level - 1))
                            if level < LEVELS - 1:
                                lower(level + 1)
                            pool.wait_ge(hl_exp.sem, hl_exp.after(layer, level + 1))
                            pool.tensor_tensor(cols(H[level % 2], level, 0), cols(HEXP[level % 2], level, 0), cols(HKT, level, 0),
                                               ALU.mult).then_inc(hl_k.step(), 1)
                        for level in range(LEVELS):
                            for n in range(NT):
                                if level == 0:
                                    pool.wait_ge(gc_a.sem, gc_a.after(layer, n + 1))
                                    pool.tensor_tensor(GA[:, n], GA[:, n], nh(G_BETA, n), ALU.mult).then_inc(p_step.step(), 1)
                                    pool.wait_ge(p_step.sem, p_step.now(layer))
                                elif level == 1:
                                    pool.wait_ge(gi_up.sem, gi_up.after(layer, n + 1))
                                else:
                                    pool.wait_ge(gi_z.sem, gi_z.after(layer, 4 * (level - 1) + n + 1))
                                mask = MC[:, C_M + level:C_M + level + 1, :].to_broadcast([P, HEADS, P])
                                pool.tensor_tensor(GAM[:, n], GA[:, n], mask, ALU.mult).then_inc(gi_mask.step(), 1)
                        for m in range(KT):
                            square(layer, 1, m)
                    with pool.Fori(0, FT // 2) as i:
                        for j in range(2):
                            pool.wait_ge(gated.sem, gated.after(layer, FT * f + j + 1, i, 2))
                            a = act_hi[:, bass.ds(i * 2 + j, 1), :]
                            pool.tensor_copy(a, tmpB[:, j:j + 1, :]).then_inc(act_h.step(FT // 2), 1)
                            pool.wait_ge(act_h.sem, act_h.after(layer, FT * f + j + 1, i, 2))
                            pool.tensor_tensor(act_lo[:, bass.ds(i * 2 + j, 1), :], tmpB[:, j:j + 1, :], a.bitcast(F32),
                                                             ALU.subtract).then_inc(act_split.step(FT // 2), 1)
                    square(layer, 2 * f, 0)
                    with pool.Fori(0, KT - 1) as i:
                        square(layer, 2 * f, 1, i, KT - 1)

        for s in used:
            if PER_LAYER:
                assert s.seen == s.n, (s.name, s.seen, s.n)
        return {s.name: s.seen for s in used}


def laid_out(a):
    L = DEPTH
    col = lambda v: np.moveaxis(v.reshape(v.shape[:-1] + (-1, P)), -1, 0)
    ins = {"x": np.ascontiguousarray(np.moveaxis(a["x"][0].reshape(T, KT, P), 0, -1).transpose(1, 0, 2)), "c": col(a["c"][0])}

    prm = np.zeros((P, L, NQ), np.float32)
    for l in range(L):
        n = (l + 1) % L
        for i, name in enumerate(("ffn1_norm", "mix_norm", "ffn2_norm")):
            prm[:, l, Q_GAIN + 8 * i:Q_GAIN + 8 * i + 8] = col(a[name][l])
        prm[:, l, Q_ADAB:Q_ADAB + 56] = col(a["ada_b"][l, 2 * DM:])
        prm[:, l, Q_ADAB + 56:Q_ADAB + 72] = col(a["ada_b"][n, :2 * DM])
        conv = a["gdn_conv_w"][l].reshape(4, 12, P)[:, [4, 5, 6, 7, 0, 1, 2, 3, 8, 9, 10, 11]]
        prm[:, l, Q_CONV:Q_CONV + 48] = conv.transpose(2, 1, 0).reshape(P, 48)
        prm[:, l, Q_SB] = np.tile(a["sb_out_norm"][l], 2)
        prm[:, l, Q_GD] = a["gdn_out_norm"][l]
        prm[:, l, Q_HG] = np.tile(a["hg_out_norm"][l], 2)
        prm[:, l, Q_AL:Q_AL + 4] = a["gdn_A_log"][l]
        prm[:, l, Q_DT:Q_DT + 4] = a["gdn_dt_bias"][l]
        prm[:, l, Q_FL] = l > 0
        prm[:, l, Q_NEG] = 0 if l > 0 else -BIG
    ins["prm"], ins["consts"] = prm, constants()
    ins["lb_logits"] = np.broadcast_to(a["hg_lb_logits"].reshape(1, L * 256), (P, L * 256))
    ins["final_gain"] = col(a["final_norm"])

    w = a["ada_w"].reshape(L, 4, 2, P, 18, 512)
    w = np.concatenate([w[..., 4:, :], np.roll(w, -1, 0)[..., :4, :]], axis=-2)
    ins["ada_w"] = w.transpose(0, 4, 1, 3, 2, 5).reshape(L, ADA_GROUPS, 4, P, W8)

    w = np.stack([a["ffn1_w_in"], a["ffn2_w_in"]], 1).reshape(L, 2, KT, P, 2, FT, P)
    ins["ffn_in"] = w.transpose(0, 1, 5, 4, 3, 2, 6).reshape(L, 2, 2 * FT, P, W8)
    w = np.stack([a["ffn1_w_out"], a["ffn2_w_out"]], 1).reshape(L, 2, 2, HALF_FT, P, KT, P)
    ins["ffn_out"] = w.transpose(0, 1, 5, 2, 4, 3, 6).reshape(L, 2, 2 * KT, P, W11)

    w = a["mix_w_in"]
    take = lambda *cuts: np.concatenate([w[..., b:e] for b, e in cuts], -1)
    feat = take((1280, 1792), (768, 1280), (1792, 2304), (2304, 2816), (2824, 3080), (3592, 3848), (0, 256), (256, 512))
    ins["mix_feat"] = feat.reshape(L, KT, P, FEAT_UNITS, P).transpose(0, 3, 2, 1, 4).reshape(L, FEAT_UNITS, P, W8)
    for name, cols in (("mix_ta", take((3080, 3336), (3336, 3592))), ("mix_tb", take((512, 768), (2816, 2824)))):
        n = cols.shape[-1]
        ins[name] = cols.reshape(L, 4, 2, P, n).transpose(0, 1, 3, 2, 4).reshape(L, 4, P, 2 * n)
    ins["mix_out"] = a["mix_w_out"].reshape(L, KT, P, KT, P).transpose(0, 3, 2, 1, 4).reshape(L, KT, P, W8)
    return {k: np.ascontiguousarray(v) for k, v in ins.items()}


def kernel(**inputs):
    import concourse.bacc as bacc
    from concourse.bass_utils import run_bass_kernel_spmd

    arrays = laid_out({k: np.asarray(v) for k, v in inputs.items()})
    nc = bacc.Bacc("TRN2", target_bir_lowering=False, num_devices=1)
    args = {k: nc.dram_tensor(f"in_{k}", v.shape, F32, kind="ExternalInput").ap() for k, v in arrays.items()}
    out = nc.dram_tensor("out", (P, KT, T), F32, kind="ExternalOutput").ap()
    build(nc, out=out, **args)
    r = run_bass_kernel_spmd(nc, [{f"in_{k}": v for k, v in arrays.items()}], core_ids=[0])
    y = r.results[0]["out"]
    return np.ascontiguousarray(y.transpose(2, 1, 0).reshape(1, T, DM))
```
